# Optimizing a Trainium2 kernel written in Bass

```python
import math
import jax, jax.numpy as jnp
from jax import lax
import numpy as np

D_MODEL = 1024
BATCH = 1
SEQ = 2048
DEPTH = 2

CHUNK = 64
MEM_LEN = 256
HEAD_DIM = 64
EPS = 1e-6
A_HEADS = 8
A_KV_HEADS = 2
A_WINDOW = 128
A_WIN_CHUNKS = A_WINDOW // CHUNK
B_HEADS = 8
SB_BLOCK = 128
C_HEADS = 16
C_KV_LATENT = 256
IDX_HEADS = 8
IDX_DIM = 64
C_TOPK_MAX = 256
C_BLOCK = 128
M_HEADS = 4

A_W = A_HEADS * HEAD_DIM
A_KVW = A_KV_HEADS * HEAD_DIM
B_W = B_HEADS * HEAD_DIM
C_W = C_HEADS * HEAD_DIM
M_W = M_HEADS * HEAD_DIM
EVEN_SPLITS = (A_W, A_KVW, A_KVW, A_W, B_W, B_W, B_W, B_W, M_W, M_W)
EVEN_IN = sum(EVEN_SPLITS)
EVEN_OUT = A_W + B_W + M_W
ODD_SPLITS = (C_W, C_KV_LATENT, IDX_HEADS * IDX_DIM, IDX_DIM, IDX_HEADS, C_W, M_W, M_W)
ODD_IN = sum(ODD_SPLITS)
ODD_OUT = C_W + M_W
N_EVEN = (DEPTH + 1) // 2
N_ODD = DEPTH // 2

kernel_name = 'hybrid_swa_stickbreak_dsa_memory_trunk'

def rmsnorm(x, g):
    xf = x.astype(jnp.float32)
    y = xf * lax.rsqrt(jnp.mean(xf * xf, axis=-1, keepdims=True) + EPS)
    return (y * g.astype(jnp.float32)).astype(x.dtype)

def alibi_slopes(n):
    return 2.0 ** (-8.0 * jnp.arange(1, n + 1, dtype=jnp.float32) / n)

def split_cols(t, sizes):
    out, off = [], 0
    for s in sizes:
        out.append(t[..., off:off + s])
        off += s
    return out

def sliding_window_sink_attention(q, k, v, sinks):
    B, S = q.shape[:2]
    nc = S // CHUNK
    g = A_HEADS // A_KV_HEADS
    W = A_WIN_CHUNKS * CHUNK
    qc = q.reshape(B, nc, CHUNK, A_KV_HEADS, g, HEAD_DIM)
    kc = k.reshape(B, nc, CHUNK, A_KV_HEADS, HEAD_DIM)
    vc = v.reshape(B, nc, CHUNK, A_KV_HEADS, HEAD_DIM)
    pad = ((0, 0), (A_WIN_CHUNKS - 1, 0), (0, 0), (0, 0), (0, 0))
    kp, vp = jnp.pad(kc, pad), jnp.pad(vc, pad)
    kb = jnp.concatenate([kp[:, i:i + nc] for i in range(A_WIN_CHUNKS)], axis=2)
    vb = jnp.concatenate([vp[:, i:i + nc] for i in range(A_WIN_CHUNKS)], axis=2)
    s = jnp.einsum('bcqhgd,bckhd->bchgqk', qc, kb).astype(jnp.float32) * (HEAD_DIM ** -0.5)
    cidx = jnp.arange(nc)[:, None]
    qpos = cidx * CHUNK + jnp.arange(CHUNK)[None, :]
    kpos = (cidx - (A_WIN_CHUNKS - 1)) * CHUNK + jnp.arange(W)[None, :]
    dist = jnp.abs(qpos[:, :, None] - kpos[:, None, :]).astype(jnp.float32)
    slopes = alibi_slopes(A_HEADS).reshape(A_KV_HEADS, g)
    s = s - slopes[None, None, :, :, None, None] * dist[None, :, None, None, :, :]
    valid = (kpos >= 0)[None, :, None, None, None, :]
    s = jnp.where(valid, s, -jnp.inf)
    sink = jnp.broadcast_to(sinks.astype(jnp.float32).reshape(A_KV_HEADS, g)[None, None, :, :, None, None],
                            s.shape[:-1] + (1,))
    p = jax.nn.softmax(jnp.concatenate([s, sink], axis=-1), axis=-1)[..., :-1]
    o = jnp.einsum('bchgqk,bckhd->bcqhgd', p.astype(v.dtype), vb)
    return o.reshape(B, S, A_W)

def stick_breaking_attention(q, k, v):
    B, S = q.shape[:2]
    scale = HEAD_DIM ** -0.5
    outs = []
    for blk in range(S // SB_BLOCK):
        q0 = blk * SB_BLOCK
        L = q0 + SB_BLOCK
        z = jnp.einsum('bqhd,bkhd->bhqk', q[:, q0:L], k[:, :L]).astype(jnp.float32) * scale
        tpos = q0 + jnp.arange(SB_BLOCK)
        causal = jnp.arange(L)[None, :] < tpos[:, None]
        log_keep = jnp.where(causal, jax.nn.log_sigmoid(-z), 0.0)
        suffix = lax.cumsum(log_keep, axis=3, reverse=True) - log_keep
        a = jnp.where(causal, jnp.exp(jax.nn.log_sigmoid(z) + suffix), 0.0)
        outs.append(jnp.einsum('bhqk,bkhd->bqhd', a.astype(v.dtype), v[:, :L]))
    return jnp.concatenate(outs, axis=1).reshape(B, S, B_W)

def dsa_sparse_attention(q, c_kv, w_uk, w_uv, q_idx, k_idx, w_idx):
    B, S = q.shape[:2]
    top_k = min(C_TOPK_MAX, S // 4)
    slopes = alibi_slopes(C_HEADS)
    spos = jnp.arange(S)
    bidx = jnp.arange(B)[:, None, None]
    idx_scale = (IDX_DIM ** -0.5) * (IDX_HEADS ** -0.5)

    def block(i):
        q0 = i * C_BLOCK
        qb = lax.dynamic_slice_in_dim(q, q0, C_BLOCK, axis=1)
        qib = lax.dynamic_slice_in_dim(q_idx, q0, C_BLOCK, axis=1)
        wib = lax.dynamic_slice_in_dim(w_idx, q0, C_BLOCK, axis=1)
        tpos = q0 + jnp.arange(C_BLOCK)
        admissible = (spos[None, :] // CHUNK) <= (tpos[:, None] // CHUNK)
        isc = jax.nn.relu(jnp.einsum('bqhd,bsd->bqhs', qib, k_idx).astype(jnp.float32))
        isc = jnp.einsum('bqh,bqhs->bqs', wib.astype(jnp.float32), isc) * idx_scale
        isc = jnp.where(admissible[None], isc, -jnp.inf)
        top_val, top_idx = lax.top_k(isc, top_k)
        sel_ok = jnp.isfinite(top_val)
        c_sel = c_kv[bidx, top_idx]
        q_lat = jnp.einsum('bqhd,lhd->bqhl', qb, w_uk)
        s = jnp.einsum('bqhl,bqkl->bqhk', q_lat, c_sel).astype(jnp.float32) * (HEAD_DIM ** -0.5)
        dist = jnp.abs(tpos[None, :, None] - top_idx).astype(jnp.float32)
        s = s - slopes[None, None, :, None] * dist[:, :, None, :]
        s = jnp.where(sel_ok[:, :, None, :], s, -jnp.inf)
        p = jax.nn.softmax(s, axis=-1)
        o_lat = jnp.einsum('bqhk,bqkl->bqhl', p.astype(c_sel.dtype), c_sel)
        return jnp.einsum('bqhl,lhd->bqhd', o_lat, w_uv)

    o = lax.map(block, jnp.arange(S // C_BLOCK))
    return jnp.transpose(o, (1, 0, 2, 3, 4)).reshape(B, S, C_W)

def memory_attention(q, mem_n, w_mem_kv):
    B, M = mem_n.shape[:2]
    mk, mv = split_cols(mem_n @ w_mem_kv, (M_W, M_W))
    mk = mk.reshape(B, M, M_HEADS, HEAD_DIM)
    mv = mv.reshape(B, M, M_HEADS, HEAD_DIM)
    s = jnp.einsum('bshd,bmhd->bhsm', q, mk).astype(jnp.float32) * (HEAD_DIM ** -0.5)
    p = jax.nn.softmax(s, axis=-1)
    o = jnp.einsum('bhsm,bmhd->bshd', p.astype(mv.dtype), mv)
    return o.reshape(q.shape[0], q.shape[1], M_W)

def even_layer(x, mem, norm_g, w_in, sinks, mem_norm_g, w_mem_kv, w_out):
    B, S, _ = x.shape
    h = rmsnorm(x, norm_g)
    qa, ka, va, ga, qb, kb, vb, gb, qm, gm = split_cols(h @ w_in, EVEN_SPLITS)
    oa = sliding_window_sink_attention(qa.reshape(B, S, A_HEADS, HEAD_DIM),
                                       ka.reshape(B, S, A_KV_HEADS, HEAD_DIM),
                                       va.reshape(B, S, A_KV_HEADS, HEAD_DIM), sinks)
    ob = stick_breaking_attention(qb.reshape(B, S, B_HEADS, HEAD_DIM),
                                  kb.reshape(B, S, B_HEADS, HEAD_DIM),
                                  vb.reshape(B, S, B_HEADS, HEAD_DIM))
    om = memory_attention(qm.reshape(B, S, M_HEADS, HEAD_DIM), rmsnorm(mem, mem_norm_g), w_mem_kv)
    y = jnp.concatenate([oa * jax.nn.silu(ga), ob * jax.nn.silu(gb), om * jax.nn.silu(gm)], axis=-1)
    return x + y @ w_out

def odd_layer(x, mem, norm_g, w_in, kv_norm_g, w_uk, w_uv, mem_norm_g, w_mem_kv, w_out):
    B, S, _ = x.shape
    h = rmsnorm(x, norm_g)
    qc, ckv, qi, ki, wi, gc, qm, gm = split_cols(h @ w_in, ODD_SPLITS)
    ckv = rmsnorm(ckv, kv_norm_g)
    oc = dsa_sparse_attention(qc.reshape(B, S, C_HEADS, HEAD_DIM), ckv, w_uk, w_uv,
                              qi.reshape(B, S, IDX_HEADS, IDX_DIM), ki, wi)
    om = memory_attention(qm.reshape(B, S, M_HEADS, HEAD_DIM), rmsnorm(mem, mem_norm_g), w_mem_kv)
    y = jnp.concatenate([oc * jax.nn.silu(gc), om * jax.nn.silu(gm)], axis=-1)
    return x + y @ w_out

def setup_inputs(seed: int = 0) -> dict:
    key = jax.random.key(seed)
    ks = jax.random.split(key, 20)

    def nrm(k, shape, scale):
        return jax.random.normal(k, shape, jnp.float32) * scale

    return {
        'x': nrm(ks[0], (BATCH, SEQ, D_MODEL), 1.0),
        'mem': nrm(ks[1], (BATCH, MEM_LEN, D_MODEL), 1.0),
        'e_norm': 1.0 + nrm(ks[2], (N_EVEN, D_MODEL), 0.02),
        'e_w_in': nrm(ks[3], (N_EVEN, D_MODEL, EVEN_IN), D_MODEL ** -0.5),
        'e_sinks': nrm(ks[4], (N_EVEN, A_HEADS), 0.5),
        'e_mem_norm': 1.0 + nrm(ks[5], (N_EVEN, D_MODEL), 0.02),
        'e_w_mem_kv': nrm(ks[6], (N_EVEN, D_MODEL, 2 * M_W), D_MODEL ** -0.5),
        'e_w_out': nrm(ks[7], (N_EVEN, EVEN_OUT, D_MODEL), EVEN_OUT ** -0.5),
        'o_norm': 1.0 + nrm(ks[8], (N_ODD, D_MODEL), 0.02),
        'o_w_in': nrm(ks[9], (N_ODD, D_MODEL, ODD_IN), D_MODEL ** -0.5),
        'o_kv_norm': 1.0 + nrm(ks[10], (N_ODD, C_KV_LATENT), 0.02),
        'o_w_uk': nrm(ks[11], (N_ODD, C_KV_LATENT, C_HEADS, HEAD_DIM), C_KV_LATENT ** -0.5),
        'o_w_uv': nrm(ks[12], (N_ODD, C_KV_LATENT, C_HEADS, HEAD_DIM), C_KV_LATENT ** -0.5),
        'o_mem_norm': 1.0 + nrm(ks[13], (N_ODD, D_MODEL), 0.02),
        'o_w_mem_kv': nrm(ks[14], (N_ODD, D_MODEL, 2 * M_W), D_MODEL ** -0.5),
        'o_w_out': nrm(ks[15], (N_ODD, ODD_OUT, D_MODEL), ODD_OUT ** -0.5),
        'final_norm': 1.0 + nrm(ks[16], (D_MODEL,), 0.02),
    }

def reference(x, mem, e_norm, e_w_in, e_sinks, e_mem_norm, e_w_mem_kv, e_w_out,
              o_norm, o_w_in, o_kv_norm, o_w_uk, o_w_uv, o_mem_norm, o_w_mem_kv, o_w_out,
              final_norm):
    h = x
    for layer in range(DEPTH):
        i = layer // 2
        if layer % 2 == 0:
            h = even_layer(h, mem, e_norm[i], e_w_in[i], e_sinks[i], e_mem_norm[i],
                           e_w_mem_kv[i], e_w_out[i])
        else:
            h = odd_layer(h, mem, o_norm[i], o_w_in[i], o_kv_norm[i], o_w_uk[i], o_w_uv[i],
                          o_mem_norm[i], o_w_mem_kv[i], o_w_out[i])
    return rmsnorm(h, final_norm)


_drawn_inputs = setup_inputs


def setup_inputs(seed=0):
    import zlib

    import numpy as np

    out = dict(_drawn_inputs(seed))
    spreads = {}
    factors = {'e_sinks': 3.945,
     'e_mem_norm': 5.96,
     'o_kv_norm': 8.0,
     'o_mem_norm': 8.0,
     'final_norm': 2.862}
    for name, (base, spread) in spreads.items():
        noise = np.random.default_rng([zlib.crc32(name.encode()), seed]).standard_normal(out[name].shape)
        drawn = base * np.exp(spread * noise) if base else spread * noise
        out[name] = __import__('jax').numpy.asarray(drawn.astype(out[name].dtype))
    for name, factor in factors.items():
        out[name] = (out[name] * factor).astype(out[name].dtype)
    return out
```

```python
from contextlib import ExitStack

import concourse.bass as bass
from concourse import mybir

F32 = mybir.dt.float32
BF16 = mybir.dt.bfloat16
I32 = mybir.dt.int32
U32 = mybir.dt.uint32
ALU = mybir.AluOpType
ACT = mybir.ActivationFunctionType

P = 128
S = 2048
D = 1024
NT = S // P
HD = 64
EPS = 1e-6
MEM = 256
TOPK = 256
LAT = 256
A_HEADS, B_HEADS, C_HEADS, I_HEADS, M_HEADS = 8, 8, 16, 8, 4
SCALE = HD ** -0.5
IDX_SCALE = (HD ** -0.5) * (I_HEADS ** -0.5)
MASKED = -1.0e30
NEVER = -3.0e38
YW = 1280
BANK = 512
SIGN = 0x80000000
PIECE = 1024
PB = PIECE // P

FM0 = {"qa": 0, "ka": 4, "qb": 5, "kb": 9, "qm": 13}
FM1 = {"qc": 0, "qi": 8, "ki": 12, "qm": 13}
NFM = 15


def slopes(n):
    return [2.0 ** (-8.0 * h / n) for h in range(1, n + 1)]


def chunks(n, w):
    return [(a, min(w, n - a)) for a in range(0, n, w)]


class Scope:

    made = 0

    def __init__(self, nc):
        self.nc = nc
        self.ctx = ExitStack()
        Scope.made += 1
        self.tag = f"s{Scope.made}_"
        self.taken = []

    def __enter__(self):
        return self

    def __exit__(self, *e):
        if self.taken and e[0] is None:
            with self.nc.Block() as block:
                @block.sync
                def _(sp):
                    for s in self.taken:
                        sp.sem_clear(s)
        self.ctx.close()

    def sb(self, name, shape, dt=F32):
        return self.ctx.enter_context(self.nc.sbuf_tensor(self.tag + name, shape, dt))

    def ps(self, name, shape, dt=F32):
        return self.ctx.enter_context(self.nc.psum_tensor(self.tag + name, shape, dt))

    def sem(self, name):
        self.taken.append(self.ctx.enter_context(self.nc.semaphore(self.tag + name)))
        return self.taken[-1]

    def sems(self, name, n):
        return [self.sem(f"{name}{k}") for k in range(n)]


class Constants:
    pass


def make_constants(nc, sc, e_sinks):
    c = Constants()
    c.ident = sc.sb("ident", [P, P])
    c.identb = sc.sb("identb", [P, P], BF16)
    c.neg_dist = sc.sb("neg_dist", [P, S])
    c.causal = sc.sb("causal", [P, P], BF16)
    c.window = sc.sb("window", [P, 2 * P])
    c.zero_bias = sc.sb("zero_bias", [P, MEM])
    c.slope_a = sc.sb("slope_a", [P, A_HEADS])
    c.slope_c = sc.sb("slope_c", [P, C_HEADS])
    c.scale_m = sc.sb("scale_m", [P, M_HEADS])
    c.fm_scale0 = sc.sb("fm_scale0", [P, 16])
    c.fm_scale1 = sc.sb("fm_scale1", [P, 16])
    c.fm_one = sc.sb("fm_one", [P, 8])
    c.sink = sc.sb("sink", [P, A_HEADS])
    with Scope(nc) as st:
        ramp = st.sb("ramp", [P, S], I32)
        cleared = st.sem("cleared")
        ramp_made = st.sem("ramp_made")
        dist_made = st.sem("dist_made")
        sinks_in = st.sem("sinks_in")
        with nc.Block() as block:
            @block.gpsimd
            def _(pool):
                nc.gpsimd.iota(ramp[:], pattern=[[-1, S]], base=S - P, channel_multiplier=1).then_inc(ramp_made, 1)
                for t in (c.ident, c.identb, c.causal):
                    nc.gpsimd.memset(t[:], 0.0).then_inc(cleared, 1)
                pool.wait_ge(cleared, 3)
                for t in (c.ident, c.identb):
                    nc.gpsimd.affine_select(out=t[:], in_=t[:], compare_op=ALU.not_equal, fill=1.0, base=0,
                                            pattern=[[-1, P]], channel_multiplier=1)
                nc.gpsimd.affine_select(out=c.causal[:], in_=c.causal[:], compare_op=ALU.is_gt, fill=MASKED,
                                        base=0, pattern=[[-1, P]], channel_multiplier=1)

            @block.sync
            def _(sp):
                sp.dma_start(c.sink[:], e_sinks[0:1, :].broadcast_to([P, A_HEADS])).then_inc(sinks_in, 16)
                sp.wait_ge(sinks_in, 16)

            @block.vector
            def _(dve):
                v = nc.vector
                dve.wait_ge(ramp_made, 1)
                v.tensor_copy(c.neg_dist[:], ramp[:]).then_inc(dist_made, 1)
                dve.wait_ge(dist_made, 1)
                v.scalar_tensor_tensor(out=c.neg_dist[:], in0=c.neg_dist[:], scalar=-1.0, in1=c.neg_dist[:],
                                       op0=ALU.mult, op1=ALU.min).then_inc(dist_made, 1)
                dve.wait_ge(dist_made, 2)
                v.tensor_copy(c.window[:], c.neg_dist[:, S - 2 * P:S]).then_inc(dist_made, 1)
                dve.wait_ge(dist_made, 3)
                v.memset(c.window[0:64, 0:64], MASKED)
                v.memset(c.window[64:128, 0:128], MASKED)
                v.memset(c.window[0:64, 192:256], MASKED)
                v.memset(c.zero_bias[:], 0.0)
                for t, n in ((c.slope_a, A_HEADS), (c.slope_c, C_HEADS)):
                    for h, s in enumerate(slopes(n)):
                        v.memset(t[:, h:h + 1], s)
                v.memset(c.scale_m[:], SCALE)
                v.memset(c.fm_scale0[:, 4:16], 1.0)
                v.memset(c.fm_scale1[:, 8:16], 1.0)
                v.memset(c.fm_one[:], 1.0)
                for t, n in ((c.fm_scale0, A_HEADS), (c.fm_scale1, C_HEADS)):
                    for h, s in enumerate(slopes(n)):
                        v.memset(t[HD * (h % 2):HD * (h % 2) + HD, h // 2:h // 2 + 1], SCALE / s)
    return c


def norm_rows(nc, c, src, gain, T, W, dstT=None, out=None):
    nt, kt = T // P, W // P
    half = nt // 2
    with Scope(nc) as sc:
        x = sc.sb("x", [P, nt, W])
        g = sc.sb("g", [P, W])
        xn = sc.sb("xn", [P, 2, W])
        sq = sc.sb("sq", [P, 2, W])
        ss = sc.sb("ss", [P, nt])
        rms = sc.sb("rms", [P, nt])
        rstd = sc.sb("rstd", [P, nt])
        tp = [sc.ps(f"tp{k}", [P, max(W, BANK)]) for k in range(2)]
        x_in = sc.sems("x_in", 2)
        g_in = sc.sem("g_in")
        squared = sc.sem("squared")
        mean_made = sc.sem("mean_made")
        root_made = sc.sem("root_made")
        rstd_made = sc.sem("rstd_made")
        normed = sc.sem("normed")
        turned = sc.sem("turned")
        evacuated = sc.sem("evacuated")
        stored = sc.sems("stored", 2)
        xv = src.rearrange("(t p) d -> p t d", p=P)
        with nc.Block() as block:
            @block.sync
            def _(sp):
                for k in range(2):
                    sp.dma_start(x[:, k * half:(k + 1) * half, :], xv[:, k * half:(k + 1) * half, :]
                                 ).then_inc(x_in[k], 16)
                sp.dma_start(g[:], gain.broadcast_to([P, W])).then_inc(g_in, 16)
                if out is not None:
                    with sp.Fori(0, half) as i:
                        for k in range(2):
                            sp.wait_ge(normed, i * 2 + k + 1)
                            sp.dma_start(out[bass.ds((i * 2 + k) * P, P), :], xn[:, k, :]).then_inc(stored[k], 16)
                    for k in range(2):
                        sp.wait_ge(stored[k], 16 * (half + 1))

            @block.scalar
            def _(act):
                for t in range(nt):
                    if t % half == 0:
                        act.wait_ge(x_in[t // half], 16)
                    if t >= 2:
                        act.wait_ge(squared, t - 1)
                    nc.scalar.activation(sq[:, t % 2, :], x[:, t, :], ACT.Square, accum_out=ss[:, t:t + 1]
                                         ).then_inc(squared, 1)
                act.wait_ge(mean_made, 1)
                nc.scalar.activation(rms[:], rms[:], ACT.Sqrt).then_inc(root_made, 1)
                if dstT is not None:
                    with act.Fori(0, half) as i:
                        for k in range(2):
                            act.wait_ge(turned, i * 2 + k + 1 + 2)
                            nc.scalar.copy(dstT[:, :, bass.ds((i * 2 + k) * P, P)],
                                           tp[k][:, 0:W].rearrange("p (k t) -> p k t", k=kt)
                                           ).then_inc(evacuated, 1)

            @block.vector
            def _(dve):
                dve.wait_ge(squared, nt)
                nc.vector.tensor_scalar(rms[:], ss[:], 1.0 / W, EPS, ALU.mult, ALU.add).then_inc(mean_made, 1)
                dve.wait_ge(root_made, 1)
                nc.vector.reciprocal(rstd[:], rms[:]).then_inc(rstd_made, 1)
                dve.wait_ge(rstd_made, 1)
                dve.wait_ge(g_in, 16)
                for k in range(2):
                    dve.wait_ge(x_in[k], 16)
                if dstT is not None:
                    dve.sem_inc(turned, 2)
                else:
                    for k in range(2):
                        dve.sem_inc(stored[k], 16)
                with dve.Fori(0, half) as i:
                    for k in range(2):
                        if dstT is not None:
                            dve.wait_ge(turned, i * 2 + k + 1)
                        else:
                            dve.wait_ge(stored[k], i * 16 + 16)
                        nc.vector.scalar_tensor_tensor(
                            out=xn[:, k, :], in0=x[:, bass.ds(i * 2 + k, 1), :].rearrange("p a d -> p (a d)"),
                            scalar=rstd[:, bass.ds(i * 2 + k, 1)], in1=g[:], op0=ALU.mult, op1=ALU.mult
                        ).then_inc(normed, 1)

            if dstT is not None:
                @block.tensor
                def _(pe):
                    pe.sem_inc(evacuated, 2)
                    with pe.Fori(0, half) as i:
                        for k in range(2):
                            pe.wait_ge(normed, i * 2 + k + 1)
                            pe.wait_ge(evacuated, i * 2 + k + 1)
                            for j in range(kt):
                                last = nc.tensor.transpose(tp[k][:, j * P:(j + 1) * P], xn[:, k, j * P:(j + 1) * P],
                                                           c.ident[:])
                            last.then_inc(turned, 1)


def in_pairs(eng, n, body):
    if n // 2 > 1:
        with eng.Fori(0, n // 2) as i:
            for k in range(2):
                body(i, k)
    elif n // 2 == 1:
        for k in range(2):
            body(0, k)
    if n % 2:
        body(n // 2, 0)


def project(nc, srcT, KT, T, w_fm, nfm, fm_scale, fm_out, tm_jobs):
    gw = min(BANK, T)
    ng = T // gw
    nt = T // P
    TG = min(4, nt)
    with Scope(nc) as sc:
        w = [sc.sb(f"w{k}", [P, KT, BANK]) for k in range(2)]
        stage = [sc.sb(f"stage{k}", [P, T]) for k in range(2)]
        scale = sc.sb("scale", [P, 2])
        rows = [sc.sb(f"rows{k}", [P, TG, BANK]) for k in range(2)]
        sig = [sc.sb(f"sig{k}", [P, BANK]) for k in range(2)]
        acc = [sc.ps(f"acc{k}", [P, BANK]) for k in range(4)]
        w_in = sc.sems("w_in", 2)
        scale_set = sc.sem("scale_set")
        summed = sc.sem("summed")
        staged = sc.sem("staged")
        stored = sc.sems("stored", 2)
        sig_made = sc.sem("sig_made")
        rowed = sc.sem("rowed")
        rows_out = sc.sems("rows_out", 2)
        nrow = nt * len(tm_jobs)
        nquad = nrow // TG
        with nc.Block() as block:
            @block.sync
            def _(sp):
                def load_fm(n, k):
                    sp.dma_start(w[k][:, :, 0:P], w_fm[bass.ds(n, 1), :, :, :].rearrange("a p k m -> p (a k) m")
                                 ).then_inc(w_in[k], 16)

                for n in range(min(2, nfm)):
                    load_fm(n, n)

                def step(i, k):
                    sp.wait_ge(summed, (i * 2 + k) * ng + ng)
                    load_fm(i * 2 + k + 2, k)

                in_pairs(sp, nfm - 2, step)
                for n, (wd, _, width, _) in enumerate(tm_jobs):
                    m = nfm + n
                    sp.wait_ge(summed, ng * (m - 1) if m - 2 < nfm else ng * nfm + nt * (m - 1 - nfm))
                    sp.dma_start(w[m % 2][:, :, 0:width], wd.rearrange("(k p) n -> p k n", p=P)
                                 ).then_inc(w_in[m % 2], 16)

            @block.tensor
            def _(pe):
                pe.sem_inc(staged, ng)
                pe.sem_inc(rowed, 4)

                def step(i, k):
                    pe.wait_ge(w_in[k], i * 16 + 16)
                    for g in range(ng):
                        pe.wait_ge(staged, (i * 2 + k) * ng + g + 1)
                        for j in range(KT):
                            last = nc.tensor.matmul(acc[g][:, 0:gw], w[k][:, j, 0:P], srcT[:, j, g * gw:(g + 1) * gw],
                                                    start=(j == 0), stop=(j == KT - 1))
                        last.then_inc(summed, 1)

                in_pairs(pe, nfm, step)
                pe.wait_ge(staged, ng * nfm + ng)
                for n, (_, _, width, _) in enumerate(tm_jobs):
                    m = nfm + n
                    pe.wait_ge(w_in[m % 2], 16 * (m // 2 + 1))
                    for t in range(nt):
                        r = n * nt + t
                        pe.wait_ge(rowed, r + 1)
                        for j in range(KT):
                            last = nc.tensor.matmul(acc[r % 4][:, 0:width], srcT[:, j, t * P:(t + 1) * P],
                                                    w[m % 2][:, j, 0:width], start=(j == 0), stop=(j == KT - 1))
                        last.then_inc(summed, 1)

            @block.scalar
            def _(act):
                for k in range(2):
                    act.sem_inc(stored[k], 16)
                    act.sem_inc(rows_out[k], 16)

                def step(i, k):
                    act.wait_ge(stored[k], i * 16 + 16)
                    nc.scalar.copy(scale[:, k:k + 1], fm_scale[:, bass.ds(i * 2 + k, 1)]).then_inc(scale_set, 1)
                    act.wait_ge(scale_set, i * 2 + k + 1)
                    for g in range(ng):
                        act.wait_ge(summed, (i * 2 + k) * ng + g + 1)
                        nc.scalar.mul(stage[k][:, g * gw:(g + 1) * gw], acc[g][:, 0:gw],
                                      scale[:, k:k + 1]).then_inc(staged, 1)
                    act.wait_ge(staged, (i * 2 + k) * ng + 2 * ng)
                    act.dma_start(fm_out[bass.ds((i * 2 + k) * P, P), :], stage[k][:, :]).then_inc(stored[k], 16)

                in_pairs(act, nfm, step)
                for n, (_, od, width, silu) in enumerate(tm_jobs):
                    for t in range(nt):
                        r = n * nt + t
                        if silu:
                            act.wait_ge(summed, ng * nfm + r + 1)
                            act.wait_ge(rowed, r + 3)
                            nc.scalar.activation(sig[r % 2][:, 0:width], acc[r % 4][:, 0:width], ACT.Sigmoid
                                                 ).then_inc(sig_made, 1)
                        if r % TG == TG - 1:
                            q = r // TG
                            act.wait_ge(rowed, r + 5)
                            act.dma_start(od[(t - TG + 1) * P:(t + 1) * P, :].rearrange("(t p) n -> p t n", p=P),
                                          rows[q % 2][:, :, 0:width]).then_inc(rows_out[q % 2], 16)
                for k in range(2):
                    act.wait_ge(stored[k], 16 * ((nfm + 1 - k) // 2 + 1))
                    act.wait_ge(rows_out[k], 16 * ((nquad + 1 - k) // 2 + 1))

            @block.vector
            def _(dve):
                gates = 0
                for n, (_, _, width, silu) in enumerate(tm_jobs):
                    for t in range(nt):
                        r = n * nt + t
                        q = r // TG
                        if r % TG == 0:
                            if q == 0:
                                dve.wait_ge(summed, ng * nfm + 1)
                            dve.wait_ge(rows_out[q % 2], 16 * (q // 2 + 1))
                        dve.wait_ge(summed, ng * nfm + r + 1)
                        dst = rows[q % 2][:, r % TG, 0:width]
                        if silu:
                            gates += 1
                            dve.wait_ge(sig_made, gates)
                            nc.vector.tensor_tensor(dst, acc[r % 4][:, 0:width], sig[r % 2][:, 0:width], ALU.mult
                                                    ).then_inc(rowed, 1)
                        else:
                            nc.vector.tensor_copy(dst, acc[r % 4][:, 0:width]).then_inc(rowed, 1)


class Unit:

    def __init__(self, j, hh, b, kbs):
        self.j, self.hh, self.b, self.kbs = j, hh, b, kbs


def number(units):
    np_, ng = 0, 0
    for u in units:
        u.pieces, u.groups = [], []
        for a, n in chunks(len(u.kbs), PB):
            u.pieces.append((np_, a, n))
            np_ += 1
        for a, n in chunks(len(u.kbs), 4):
            u.groups.append((ng, a, n))
            ng += 1
    return np_, ng


def softmax_attention(nc, c, steps, per_pair, loads, NK, y_out, scale_tab, sink, bias_of, v_shared=False):
    units = [Unit(j, hh, b, kbs) for j in range(2) for hh in range(2) for b, kbs in per_pair]
    NP, NG = number(units)
    NU = len(units)
    assert NP % 2 == 0 and NG % 2 == 0 and NU % 2 == 0
    VW = HD if v_shared else 2 * HD
    KBW = max(len(u.kbs) for u in units) * P
    two = KBW > PIECE
    with Scope(nc) as sc:
        q = [sc.sb(f"q{k}", [P, S]) for k in range(2)]
        kk = [sc.sb(f"k{k}", [P, NK]) for k in range(2)]
        v = [sc.sb(f"v{k}", [P, NK // P, VW]) for k in range(2)]
        gt = [sc.sb(f"g{k}", [P, NT, 2 * HD]) for k in range(2)]
        y = [sc.sb(f"y{k}", [P, NT, 2 * HD]) for k in range(2)]
        probs = [sc.sb(f"probs{k}", [P, KBW]) for k in range(2)]
        pT = [sc.sb(f"pT{k}", [P, 4 * P]) for k in range(2)]
        mx = sc.sb("mx", [P, 2, 4])
        gate = sc.sb("gate", [P, 2])
        scales = sc.sb("scales", [P, 4])
        sinks = sc.sb("sinks", [P, 4])
        nmx = sc.sb("nmx", [P, 2])
        rsum = sc.sb("rsum", [P, 2, 2])
        rden = sc.sb("rden", [P, 2, 2])
        s_ps = [sc.ps(f"s{k}", [P, PIECE]) for k in range(2)]
        t_ps = [sc.ps(f"t{k}", [P, BANK]) for k in range(2)]
        o_ps = [sc.ps(f"o{k}", [P, BANK]) for k in range(2)]
        loaded = sc.sems("loaded", 2)
        pair_done = sc.sem("pair_done")
        y_stored = sc.sems("y_stored", 2)
        scored = sc.sem("scored")
        biased = sc.sem("biased")
        chain = sc.sem("chain")
        max_made = sc.sem("max_made")
        exp_made = sc.sem("exp_made")
        turned = sc.sem("turned")
        taken = sc.sem("taken")
        fed = sc.sem("fed")
        summed = sc.sem("summed")
        out_made = sc.sem("out_made")
        heads_set = sc.sem("heads_set")
        nload = 5 if v_shared else 4
        links = sum((1 if len(u.pieces) > 1 else 0) + (2 if sink is not None else 1)
                    + (1 if sink is not None else 0) + 1 for u in units)
        with nc.Block() as block:
            @block.sync
            def _(sp):
                sp.sem_inc(pair_done, 2)
                with sp.Fori(0, steps) as i:
                    for j in range(2):
                        sp.wait_ge(pair_done, i * 2 + j + 1)
                        qd, kds, vd, gd = loads(i, j)
                        sp.dma_start(q[j][:], qd).then_inc(loaded[j], 16)
                        w = P // len(kds)
                        for n, kd in enumerate(kds):
                            sp.dma_start(kk[j][n * w:(n + 1) * w, :], kd).then_inc(loaded[j], 16)
                        sp.dma_start(v[j][:], vd).then_inc(loaded[j], 16)
                        sp.dma_start(gt[j][:], gd).then_inc(loaded[j], 16)

            @block.tensor
            def _(pe):
                pe.sem_inc(biased, 2)
                pe.sem_inc(taken, 2)
                pe.sem_inc(out_made, 2)

                def score(i, u):
                    r = slice(HD * u.hh, HD * u.hh + HD)
                    pe.wait_ge(loaded[u.j], i * (16 * nload) + 16 * nload)
                    for n, a, m in u.pieces:
                        pe.wait_ge(biased, i * NP + n + 1)
                        for x, w in chunks(m * P, BANK):
                            k0 = (u.kbs[0] + a) * P + x
                            last = nc.tensor.matmul(s_ps[n % 2][:, x:x + w], q[u.j][r, u.b * P:(u.b + 1) * P],
                                                    kk[u.j][r, k0:k0 + w], start=True, stop=True)
                        last.then_inc(scored, 1)

                with pe.Fori(0, steps) as i:
                    score(i, units[0])
                    for ui, u in enumerate(units):
                        if ui + 1 < NU:
                            score(i, units[ui + 1])
                        pe.wait_ge(exp_made, i * NU + ui + 1)

                        def turn(n, a, m):
                            pe.wait_ge(taken, i * NG + n + 1)
                            for x in range(m):
                                last = nc.tensor.transpose(t_ps[n % 2][:, x * P:(x + 1) * P],
                                                           probs[ui % 2][:, (a + x) * P:(a + x + 1) * P], c.ident[:])
                            last.then_inc(turned, 1)

                        def feed(n, a, m):
                            if a == 0:
                                pe.wait_ge(out_made, i * NU + ui + 1)
                            pe.wait_ge(taken, i * NG + n + 3)
                            for x in range(m):
                                vc = 0 if v_shared else HD * u.hh
                                last = nc.tensor.matmul(o_ps[ui % 2][:, 0:HD], pT[n % 2][:, x * P:(x + 1) * P],
                                                        v[u.j][:, u.kbs[a + x], vc:vc + HD],
                                                        start=(a + x == 0), stop=(a + x == len(u.kbs) - 1))
                            last.then_inc(fed, 1)

                        for n, grp in enumerate(u.groups):
                            turn(*grp)
                            if n:
                                feed(*u.groups[n - 1])
                        feed(*u.groups[-1])

            @block.scalar
            def _(act):
                act.sem_inc(fed, 2)
                with act.Fori(0, steps) as i:
                    act.wait_ge(heads_set, i + 1)
                    for ui, u in enumerate(units):
                        sl = ui % 2
                        L = len(u.kbs) * P
                        h4 = u.j * 2 + u.hh
                        act.wait_ge(max_made, i * NU + ui + 1)
                        if sink is None:
                            nc.scalar.activation(probs[sl][:, 0:L], probs[sl][:, 0:L], ACT.Exp, bias=nmx[:, sl:sl + 1],
                                                 scale=scales[:, h4:h4 + 1],
                                                 accum_out=rsum[:, sl, 0:1]).then_inc(exp_made, 1)
                        else:
                            nc.scalar.activation(rsum[:, sl, 1:2], sinks[:, h4:h4 + 1], ACT.Exp,
                                                 bias=nmx[:, sl:sl + 1])
                            nc.scalar.activation(probs[sl][:, 0:L], probs[sl][:, 0:L], ACT.Exp, bias=nmx[:, sl:sl + 1],
                                                 scale=scales[:, h4:h4 + 1],
                                                 accum_out=rsum[:, sl, 0:1]).then_inc(exp_made, 1)
                        for n, a, m in u.groups:
                            act.wait_ge(fed, i * NG + n + 1)
                            act.wait_ge(turned, i * NG + n + 1)
                            nc.scalar.copy(pT[n % 2][:, 0:m * P], t_ps[n % 2][:, 0:m * P]).then_inc(taken, 1)
                        if ui in (NU // 2 + 1, NU - 1):
                            j = ui // (NU // 2 + 2)
                            act.wait_ge(pair_done, i * 2 + j + 3)
                            act.dma_start(y_out(i, j), y[j][:]).then_inc(y_stored[j], 16)
                for j in range(2):
                    act.wait_ge(y_stored[j], 16 * (steps + 1))

            @block.vector
            def _(dve):
                for j in range(2):
                    dve.sem_inc(y_stored[j], 16)

                with dve.Fori(0, steps) as i:
                    done = [0]

                    def link(ins):
                        done[0] += 1
                        ins.then_inc(chain, 1)
                        dve.wait_ge(chain, i * links + done[0])

                    def stats(ui, u):
                        sl = ui % 2
                        h4 = u.j * 2 + u.hh
                        if ui >= 2:
                            dve.wait_ge(fed, i * NG + units[ui - 2].groups[-1][0] + 3)
                        bias = bias_of(u)
                        for pn, (n, a, m) in enumerate(u.pieces):
                            dve.wait_ge(scored, i * NP + n + 1)
                            nc.vector.memset(gate[:, pn:pn + 1], 0.0)
                            ins = nc.vector.tensor_tensor_reduce(
                                out=probs[sl][:, a * P:(a + m) * P], in0=s_ps[n % 2][:, 0:m * P],
                                in1=bias[:, a * P:(a + m) * P], scale=1.0, scalar=-3.0e38, op0=ALU.add, op1=ALU.max,
                                accum_out=mx[:, sl, pn:pn + 1])
                            ins.then_inc(biased, 1)
                        dve.wait_ge(biased, i * NP + u.pieces[-1][0] + 3)
                        m0 = mx[:, sl, 0:1]
                        if len(u.pieces) > 1:
                            link(nc.vector.tensor_tensor(mx[:, sl, 2:3], mx[:, sl, 0:1], mx[:, sl, 1:2], ALU.max))
                            m0 = mx[:, sl, 2:3]
                        if sink is None:
                            nc.vector.tensor_scalar(nmx[:, sl:sl + 1], m0, scales[:, h4:h4 + 1], -1.0,
                                                    ALU.mult, ALU.mult).then_inc(max_made, 1)
                        else:
                            link(nc.vector.tensor_scalar(mx[:, sl, 3:4], m0, scales[:, h4:h4 + 1],
                                                         sinks[:, h4:h4 + 1], ALU.mult, ALU.max))
                            nc.vector.tensor_scalar(nmx[:, sl:sl + 1], mx[:, sl, 3:4], -1.0, None,
                                                    ALU.mult).then_inc(max_made, 1)

                    def output(ui, u):
                        sl = ui % 2
                        dve.wait_ge(exp_made, i * NU + ui + 1)
                        den = rsum[:, sl, 0:1]
                        if sink is not None:
                            link(nc.vector.tensor_tensor(rden[:, sl, 1:2], rsum[:, sl, 0:1], rsum[:, sl, 1:2], ALU.add))
                            den = rden[:, sl, 1:2]
                        link(nc.vector.reciprocal(rden[:, sl, 0:1], den))
                        if ui % (NU // 2) == 0:
                            dve.wait_ge(y_stored[u.j], i * 16 + 16)
                            dve.wait_ge(loaded[u.j], i * (16 * nload) + 16 * nload)
                        dve.wait_ge(fed, i * NG + u.groups[-1][0] + 3)
                        cc = slice(HD * u.hh, HD * u.hh + HD)
                        last = nc.vector.scalar_tensor_tensor(
                            out=y[u.j][:, u.b, cc], in0=o_ps[sl][:, 0:HD], scalar=rden[:, sl, 0:1],
                            in1=gt[u.j][:, u.b, cc], op0=ALU.mult, op1=ALU.mult).then_inc(out_made, 1)
                        if ui % (NU // 2) == NU // 2 - 1:
                            dve.wait_ge(out_made, i * NU + ui + 3)
                            dve.sem_inc(pair_done, 1)

                    if sink is not None:
                        nc.vector.tensor_copy(sinks[:], sink[:, bass.ds(i * 4, 4)])
                    nc.vector.tensor_copy(scales[:], scale_tab[:, bass.ds(i * 4, 4)]).then_inc(heads_set, 1)
                    dve.wait_ge(heads_set, i + 1)
                    stats(0, units[0])
                    for ui, u in enumerate(units):
                        if ui + 1 < NU:
                            stats(ui + 1, units[ui + 1])
                        output(ui, u)
                    assert done[0] <= links
                    if done[0] < links:
                        dve.sem_inc(chain, links - done[0])


def stick_breaking(nc, c, fm, vals, gates, y_dram):
    steps = B_HEADS // 4
    units = []
    for j in range(2):
        for hh in range(2):
            for b in range(NT):
                ps = chunks(b + 1, PB)
                for n, (a, m) in enumerate(reversed(ps)):
                    units.append((j, hh, b, a, m, n == 0, n == len(ps) - 1))
    NU = len(units)
    groups, outs = [], []
    ng = no = 0
    for j, hh, b, a, m, first, last in units:
        groups.append([(ng + n, x, w) for n, (x, w) in enumerate(chunks(m, 4))])
        ng += len(groups[-1])
        outs.append(no)
        no += last
    NG, NO = ng, no
    R = 4
    assert NU % R == 0 and NG % 2 == 0 and NO % 2 == 0
    with Scope(nc) as sc:
        q = [sc.sb(f"q{k}", [P, S]) for k in range(2)]
        kk = [sc.sb(f"k{k}", [P, S]) for k in range(2)]
        v = [sc.sb(f"v{k}", [P, NT, 2 * HD]) for k in range(2)]
        gt = [sc.sb(f"g{k}", [P, NT, 2 * HD]) for k in range(2)]
        y = [sc.sb(f"y{k}", [P, NT, 2 * HD]) for k in range(2)]
        beta = [sc.sb(f"beta{k}", [P, PIECE]) for k in range(R)]
        keep = [sc.sb(f"keep{k}", [P, PIECE]) for k in range(R)]
        left = [sc.sb(f"left{k}", [P, PIECE + 8]) for k in range(R)]
        pT = [sc.sb(f"pT{k}", [P, 4 * P]) for k in range(2)]
        z_ps = [sc.ps(f"z{k}", [P, PIECE]) for k in range(2)]
        t_ps = [sc.ps(f"t{k}", [P, BANK]) for k in range(2)]
        o_ps = [sc.ps(f"o{k}", [P, BANK]) for k in range(2)]
        loaded = sc.sems("loaded", 2)
        pair_done = sc.sem("pair_done")
        y_stored = sc.sems("y_stored", 2)
        scored = sc.sem("scored")
        squashed = sc.sem("squashed")
        edge = sc.sem("edge")
        scanned = sc.sem("scanned")
        weighed = sc.sem("weighed")
        turned = sc.sem("turned")
        taken = sc.sem("taken")
        fed = sc.sem("fed")
        out_made = sc.sem("out_made")
        fed_after = [g[-1][0] + 1 for g in groups]

        with nc.Block() as block:
            @block.sync
            def _(sp):
                sp.sem_inc(pair_done, 2)
                with sp.Fori(0, steps) as i:
                    for j in range(2):
                        pair = i * 2 + j
                        sp.wait_ge(pair_done, pair + 1)
                        sp.dma_start(q[j][:], fm[bass.ds((pair + FM0["qb"]) * P, P), :]).then_inc(loaded[j], 16)
                        sp.dma_start(kk[j][:], fm[bass.ds((pair + FM0["kb"]) * P, P), :]).then_inc(loaded[j], 16)
                        for t, d in ((v[j], vals), (gt[j], gates)):
                            sp.dma_start(t[:], d.rearrange("(t p) n -> p t n", p=P)[:, :, bass.ds(pair * P, P)]
                                         ).then_inc(loaded[j], 16)

            @block.tensor
            def _(pe):
                pe.sem_inc(squashed, 2)
                pe.sem_inc(taken, 2)
                pe.sem_inc(out_made, 2)

                def score(i, ui):
                    j, hh, b, a, m, first, last = units[ui]
                    r = slice(HD * hh, HD * hh + HD)
                    pe.wait_ge(loaded[j], i * 64 + 64)
                    pe.wait_ge(squashed, i * NU + ui + 1)
                    for x, w in chunks(m * P, BANK):
                        diag = first and x + w == m * P
                        ins = nc.tensor.matmul(z_ps[ui % 2][:, x:x + w], q[j][r, b * P:(b + 1) * P],
                                               kk[j][r, a * P + x:a * P + x + w], start=True, stop=not diag)
                        if diag:
                            ins = nc.tensor.matmul(z_ps[ui % 2][:, x + w - P:x + w], c.identb[:], c.causal[:],
                                                   start=False, stop=True)
                    ins.then_inc(scored, 1)

                with pe.Fori(0, steps) as i:
                    score(i, 0)
                    score(i, 1)
                    for ui, (j, hh, b, a, m, first, last) in enumerate(units):
                        if ui + 2 < NU:
                            score(i, ui + 2)
                        pe.wait_ge(weighed, i * NU + ui + 1)

                        def turn(n, x, w):
                            pe.wait_ge(taken, i * NG + n + 1)
                            for e in range(w):
                                ins = nc.tensor.transpose(t_ps[n % 2][:, e * P:(e + 1) * P],
                                                          beta[ui % R][:, (x + e) * P:(x + e + 1) * P], c.ident[:])
                            ins.then_inc(turned, 1)

                        def feed(n, x, w):
                            if first and x == 0:
                                pe.wait_ge(out_made, i * NO + outs[ui] + 1)
                            pe.wait_ge(taken, i * NG + n + 3)
                            for e in range(w):
                                ins = nc.tensor.matmul(o_ps[outs[ui] % 2][:, 0:HD], pT[n % 2][:, e * P:(e + 1) * P],
                                                       v[j][:, a + x + e, HD * hh:HD * hh + HD],
                                                       start=(first and x + e == 0), stop=(last and x + e == m - 1))
                            ins.then_inc(fed, 1)

                        for n, grp in enumerate(groups[ui]):
                            turn(*grp)
                            if n:
                                feed(*groups[ui][n - 1])
                        feed(*groups[ui][-1])

            @block.scalar
            def _(act):
                act.sem_inc(fed, 2)

                with act.Fori(0, steps) as i:
                    def squash(ui):
                        j, hh, b, a, m, first, last = units[ui]
                        act.wait_ge(scored, i * NU + ui + 1)
                        if ui >= R:
                            act.wait_ge(fed, i * NG + fed_after[ui - R] + 2)
                        nc.scalar.activation(beta[ui % R][:, 0:m * P], z_ps[ui % 2][:, 0:m * P], ACT.Sigmoid,
                                             scale=SCALE)
                        nc.scalar.activation(keep[ui % R][:, 0:m * P], z_ps[ui % 2][:, 0:m * P], ACT.Sigmoid,
                                             scale=-SCALE).then_inc(squashed, 1)

                    squash(0)
                    squash(1)
                    for ui in range(NU):
                        if ui + 2 < NU:
                            squash(ui + 2)
                        for n, x, w in groups[ui]:
                            act.wait_ge(fed, i * NG + n + 1)
                            act.wait_ge(turned, i * NG + n + 1)
                            nc.scalar.copy(pT[n % 2][:, 0:w * P], t_ps[n % 2][:, 0:w * P]).then_inc(taken, 1)
                        if ui in (NU // 2 + 1, NU - 1):
                            j = ui // (NU // 2 + 2)
                            act.wait_ge(pair_done, i * 2 + j + 3)
                            act.dma_start(token_view(y_dram, (i * 2 + j) * P + A_HEADS * HD, P), y[j][:]
                                          ).then_inc(y_stored[j], 16)
                for j in range(2):
                    act.wait_ge(y_stored[j], 16 * (steps + 1))

            @block.gpsimd
            def _(pool):
                with pool.Fori(0, steps) as i:
                    for ui, (j, hh, b, a, m, first, last) in enumerate(units):
                        pool.wait_ge(scanned, i * NU + ui + 1)
                        nc.gpsimd.tensor_tensor(beta[ui % R][:, 0:m * P], beta[ui % R][:, 0:m * P],
                                                left[ui % R][:, 1:m * P + 1], ALU.mult).then_inc(weighed, 1)

            @block.vector
            def _(dve):
                for j in range(2):
                    dve.sem_inc(y_stored[j], 16)

                with dve.Fori(0, steps) as i:
                    def scan(ui):
                        j, hh, b, a, m, first, last = units[ui]
                        w = m * P
                        if ui >= R:
                            dve.wait_ge(weighed, i * NU + ui - R + 1)
                        dst = left[ui % R]
                        if first:
                            ins = nc.vector.memset(dst[:, w:w + 1], 1.0)
                        else:
                            dve.wait_ge(scanned, i * NU + ui)
                            ins = nc.vector.tensor_copy(dst[:, w:w + 1], left[(ui - 1) % R][:, 0:1])
                        ins.then_inc(edge, 1)
                        dve.wait_ge(edge, i * NU + ui + 1)
                        dve.wait_ge(squashed, i * NU + ui + 3)
                        kr = keep[ui % R][:, 0:w][:, ::-1]
                        nc.vector.tensor_tensor_scan(out=dst[:, 0:w][:, ::-1], data0=kr, data1=kr,
                                                     initial=dst[:, w:w + 1], op0=ALU.mult, op1=ALU.min
                                                     ).then_inc(scanned, 1)

                    def output(ui):
                        j, hh, b, a, m, first, last = units[ui]
                        if ui % (NU // 2) == NT // NT - 1:
                            dve.wait_ge(y_stored[j], i * 16 + 16)
                            dve.wait_ge(loaded[j], i * 64 + 64)
                        if last:
                            dve.wait_ge(fed, i * NG + fed_after[ui] + 2)
                            cc = slice(HD * hh, HD * hh + HD)
                            nc.vector.tensor_tensor(y[j][:, b, cc], o_ps[outs[ui] % 2][:, 0:HD], gt[j][:, b, cc],
                                                    ALU.mult).then_inc(out_made, 1)
                        if ui % (NU // 2) == NU // 2 - 1:
                            dve.wait_ge(out_made, i * NO + outs[ui] + 3)
                            dve.sem_inc(pair_done, 1)

                    scan(0)
                    scan(1)
                    for ui in range(NU):
                        if ui + 2 < NU:
                            scan(ui + 2)
                        output(ui)


def index_scores(nc, c, fm, wi, scores):
    units = [(j, hh, b, a, m) for j in range(2) for hh in range(2) for b in range(2, NT)
             for a, m in chunks(b + 1, PB)]
    NU = len(units)
    per_head = NU // 4
    steps = I_HEADS // 4
    assert NU % 4 == 0
    with Scope(nc) as sc:
        q = [sc.sb(f"q{k}", [P, S]) for k in range(2)]
        kk = sc.sb("k", [P, S])
        w_raw = sc.sb("w_raw", [P, NT, I_HEADS])
        w = sc.sb("w", [P, NT, I_HEADS])
        pos = [sc.sb(f"pos{k}", [P, PIECE]) for k in range(4)]
        s_ps = [sc.ps(f"s{k}", [P, PIECE]) for k in range(4)]
        loaded = sc.sems("loaded", 2)
        keys_in = sc.sem("keys_in")
        w_in = sc.sem("w_in")
        w_made = sc.sem("w_made")
        scored = sc.sem("scored")
        clipped = sc.sem("clipped")
        added = sc.sem("added")
        with nc.Block() as block:
            @block.sync
            def _(sp):
                sp.dma_start(w_raw[:], wi.rearrange("(t p) n -> p t n", p=P)).then_inc(w_in, 16)
                for r in range(2):
                    sp.dma_start(kk[r * HD:(r + 1) * HD, :], fm[FM1["ki"] * P:FM1["ki"] * P + HD, :]
                                 ).then_inc(keys_in, 16)
                sp.sem_inc(scored, NU)
                with sp.Fori(0, steps) as i:
                    for j in range(2):
                        sp.wait_ge(scored, i * NU + (j + 1) * (NU // 2))
                        sp.dma_start(q[j][:], fm[bass.ds((i * 2 + j + FM1["qi"]) * P, P), :]).then_inc(loaded[j], 16)

            @block.tensor
            def _(pe):
                pe.sem_inc(clipped, 4)
                pe.wait_ge(keys_in, 32)
                with pe.Fori(0, steps) as i:
                    for ui, (j, hh, b, a, m) in enumerate(units):
                        r = slice(HD * hh, HD * hh + HD)
                        if ui % (NU // 2) == 0:
                            pe.wait_ge(loaded[j], i * 16 + 16)
                        pe.wait_ge(clipped, i * NU + ui + 1)
                        for x, wd in chunks(m * P, BANK):
                            last = nc.tensor.matmul(s_ps[ui % 4][:, x:x + wd], q[j][r, b * P:(b + 1) * P],
                                                    kk[r, a * P + x:a * P + x + wd], start=True, stop=True)
                        last.then_inc(scored, 1)

            @block.scalar
            def _(act):
                with act.Fori(0, steps) as i:
                    for ui, (j, hh, b, a, m) in enumerate(units):
                        act.wait_ge(scored, i * NU + ui + 1 + NU)
                        act.wait_ge(added, i * NU + ui + 1 + per_head)
                        nc.scalar.activation(pos[ui % 4][:, 0:m * P], s_ps[ui % 4][:, 0:m * P], ACT.Relu
                                             ).then_inc(clipped, 1)

            @block.vector
            def _(dve):
                for b in range(2, NT):
                    nc.vector.memset(scores(b), 0.0)
                dve.wait_ge(w_in, 16)
                nc.vector.tensor_scalar(w[:], w_raw[:], IDX_SCALE, None, ALU.mult).then_inc(w_made, 1)
                dve.wait_ge(w_made, 1)
                dve.sem_inc(added, 4 + per_head)
                with dve.Fori(0, steps) as i:
                    for ui, (j, hh, b, a, m) in enumerate(units):
                        dst = scores(b)[:, a * P:(a + m) * P]
                        dve.wait_ge(clipped, i * NU + ui + 5)
                        dve.wait_ge(added, i * NU + ui + 5)
                        nc.vector.scalar_tensor_tensor(
                            out=dst, in0=pos[ui % 4][:, 0:m * P],
                            scalar=w[:, b, bass.ds(i * 4 + j * 2 + hh, 1)], in1=dst, op0=ALU.mult, op1=ALU.add
                        ).then_inc(added, 1)


def select_keys(nc, c, scores, all_scores):
    B0 = TOPK // P
    NB = NT - B0
    with Scope(nc) as sc:
        junk = [sc.sb(f"junk{k}", [P, S], BF16) for k in range(2)]
        even = sc.sb("even", [P, S])
        rank = sc.sb("rank", [P, S])
        best = sc.sb("best", [P, NB], U32)
        bit = sc.sb("bit", [P, NB], U32)
        cand = sc.sb("cand", [P, NB], U32)
        flip = sc.sb("flip", [P, NB], U32)
        thr = sc.sb("thr", [P, NB], U32)
        cnt = sc.sb("cnt", [P, NB])
        enough = sc.sb("enough", [P, NB], U32)
        room = sc.sb("room", [P, NB])
        ch = sc.sem("ch")
        counted = sc.sem("counted")
        pre = sc.sem("pre")
        post = sc.sem("post")
        PER = 6
        with nc.Block() as block:
            @block.vector
            def _(dve):
                v = nc.vector
                for b in range(NT):
                    L = (b + 1) * P
                    if b < B0:
                        v.tensor_copy(scores(b), c.neg_dist[:, S - L:S]).then_inc(pre, 1)
                        dve.wait_ge(pre, b + 1)
                    v.memset(scores(b)[0:HD, L - HD:L], MASKED if b < B0 else NEVER).then_inc(post, 1)
                dve.wait_ge(post, NT)
                v.memset(best[:], 0)
                v.memset(bit[:], SIGN).then_inc(pre, 1)
                dve.wait_ge(pre, B0 + 1)

                def as_float(i, n, src):
                    v.tensor_scalar(flip[:], src[:], 31, 0xFFFFFFFF, ALU.arith_shift_right, ALU.bitwise_xor
                                    ).then_inc(ch, 1)
                    dve.wait_ge(ch, i * PER + n + 1)
                    v.tensor_scalar(flip[:], flip[:], SIGN, None, ALU.bitwise_or).then_inc(ch, 1)
                    dve.wait_ge(ch, i * PER + n + 2)
                    v.tensor_tensor(thr[:], src[:], flip[:], ALU.bitwise_xor).then_inc(ch, 1)
                    dve.wait_ge(ch, i * PER + n + 3)

                with dve.Fori(0, 32) as i:
                    v.tensor_tensor(cand[:], best[:], bit[:], ALU.bitwise_or).then_inc(ch, 1)
                    dve.wait_ge(ch, i * PER + 1)
                    as_float(i, 1, cand)
                    for n in range(NB):
                        b = n + B0
                        if n >= 2:
                            dve.wait_ge(counted, i * NB + n - 1)
                        v.tensor_scalar(junk[n % 2][:, 0:(b + 1) * P], scores(b), thr[:, n:n + 1].bitcast(F32),
                                        None, ALU.is_ge, ALU.add, accum_out=cnt[:, n:n + 1]).then_inc(counted, 1)
                    dve.wait_ge(counted, i * NB + NB)
                    v.tensor_scalar(enough[:], cnt[:], TOPK - 0.5, None, ALU.is_ge).then_inc(ch, 1)
                    dve.wait_ge(ch, i * PER + 5)
                    v.tensor_scalar(bit[:], bit[:], 1, None, ALU.logical_shift_right)
                    v.copy_predicated(best[:], enough[:], cand[:]).then_inc(ch, 1)
                    dve.wait_ge(ch, i * PER + 6)
                as_float(32, 0, best)
                base = 32 * PER + 3
                for n in range(NB):
                    b = n + B0
                    L = (b + 1) * P
                    t = thr[:, n:n + 1].bitcast(F32)
                    sc_b = scores(b)
                    v.tensor_scalar(junk[0][:, 0:L], sc_b, t, None, ALU.is_gt, ALU.add, accum_out=cnt[:, n:n + 1])
                    v.tensor_scalar(even[:, 0:L], sc_b, t, None, ALU.is_equal).then_inc(ch, 1)
                    base += 1
                    dve.wait_ge(ch, base)
                    v.tensor_scalar(room[:, n:n + 1], cnt[:, n:n + 1], -1.0, float(TOPK), ALU.mult, ALU.add)
                    v.tensor_tensor_scan(out=rank[:, 0:L], data0=even[:, 0:L], data1=even[:, 0:L], initial=0.0,
                                         op0=ALU.add, op1=ALU.max).then_inc(ch, 1)
                    base += 1
                    dve.wait_ge(ch, base)
                    v.scalar_tensor_tensor(out=even[:, 0:L], in0=rank[:, 0:L], scalar=room[:, n:n + 1],
                                           in1=even[:, 0:L], op0=ALU.is_le, op1=ALU.mult).then_inc(ch, 1)
                    base += 1
                    dve.wait_ge(ch, base)
                    v.scalar_tensor_tensor(out=rank[:, 0:L], in0=sc_b, scalar=t, in1=even[:, 0:L],
                                           op0=ALU.is_gt, op1=ALU.add).then_inc(ch, 1)
                    base += 1
                    dve.wait_ge(ch, base)
                    v.tensor_scalar(even[:, 0:L], rank[:, 0:L], -1.0, -MASKED, ALU.add, ALU.mult).then_inc(ch, 1)
                    base += 1
                    dve.wait_ge(ch, base)
                    v.tensor_tensor(sc_b, even[:, 0:L], c.neg_dist[:, S - L:S], ALU.add).then_inc(ch, 1)
                    base += 1
                    dve.wait_ge(ch, base)


def out_project(nc, c, y_dram, w_out, resid, dst):
    KY = YW // P
    half = NT // 2
    with Scope(nc) as sc:
        w = sc.sb("w", [P, KY, D])
        y = [sc.sb(f"y{k}", [P, YW]) for k in range(2)]
        x = [sc.sb(f"x{k}", [P, D]) for k in range(2)]
        h = [sc.sb(f"h{k}", [P, D]) for k in range(2)]
        yT = [sc.sb(f"yT{k}", [P, YW]) for k in range(2)]
        t_ps = sc.ps("t", [P, 3 * BANK])
        o_ps = [sc.ps(f"o{k}", [P, D]) for k in range(2)]
        w_in = sc.sem("w_in")
        y_in = sc.sems("y_in", 2)
        x_in = sc.sems("x_in", 2)
        turned = sc.sem("turned")
        taken = sc.sem("taken")
        summed = sc.sem("summed")
        added = sc.sem("added")
        stored = sc.sems("stored", 2)
        with nc.Block() as block:
            @block.sync
            def _(sp):
                sp.dma_start(w[:], w_out.rearrange("(k p) n -> p k n", p=P)).then_inc(w_in, 16)

                def load(n, k, d, to, arrived):
                    sp.dma_start(to[k][:], d[bass.ds(n * P, P), :]).then_inc(arrived[k], 16)

                def store(n, k):
                    sp.dma_start(dst[bass.ds(n * P, P), :], h[k][:]).then_inc(stored[k], 16)

                for k in range(2):
                    load(k, k, y_dram, y, y_in)
                    load(k, k, resid, x, x_in)
                with sp.Fori(0, half - 1) as i:
                    for k in range(2):
                        n = i * 2 + k + 2
                        sp.wait_ge(turned, n + 1)
                        load(n, k, y_dram, y, y_in)
                        sp.wait_ge(added, n + 1)
                        load(n, k, resid, x, x_in)
                        store(n - 2, k)
                for k in range(2):
                    sp.wait_ge(added, NT + k + 1)
                    store(NT - 2 + k, k)
                    sp.wait_ge(stored[k], 16 * (half + 1))

            @block.tensor
            def _(pe):
                pe.sem_inc(turned, 2)
                pe.sem_inc(taken, 1)

                def turn(i, k):
                    pe.wait_ge(y_in[k], i * 16 + 16)
                    pe.wait_ge(taken, i * 2 + k + 1)
                    for j in range(KY):
                        last = nc.tensor.transpose(t_ps[:, j * P:(j + 1) * P], y[k][:, j * P:(j + 1) * P], c.ident[:])
                    last.then_inc(turned, 1)

                def product(i, k):
                    pe.wait_ge(taken, i * 2 + k + 2)
                    pe.wait_ge(added, i * 2 + k + 1)
                    for x0 in range(0, D, BANK):
                        for j in range(KY):
                            last = nc.tensor.matmul(o_ps[k][:, x0:x0 + BANK], yT[k][:, j * P:(j + 1) * P],
                                                    w[:, j, x0:x0 + BANK], start=(j == 0), stop=(j == KY - 1))
                    last.then_inc(summed, 1)

                turn(0, 0)
                pe.wait_ge(w_in, 16)
                with pe.Fori(0, half - 1) as i:
                    turn(i, 1)
                    product(i, 0)
                    turn(i + 1, 0)
                    product(i, 1)
                turn(half - 1, 1)
                product(half - 1, 0)
                product(half - 1, 1)

            @block.scalar
            def _(act):
                act.sem_inc(summed, 2)
                with act.Fori(0, half) as i:
                    for k in range(2):
                        n = i * 2 + k
                        act.wait_ge(summed, n + 1)
                        act.wait_ge(turned, n + 3)
                        nc.scalar.copy(yT[k][:], t_ps[:, 0:YW]).then_inc(taken, 1)

            @block.vector
            def _(dve):
                dve.sem_inc(added, 2)
                for k in range(2):
                    dve.sem_inc(stored[k], 16)
                with dve.Fori(0, half) as i:
                    for k in range(2):
                        n = i * 2 + k
                        dve.wait_ge(summed, n + 3)
                        dve.wait_ge(x_in[k], i * 16 + 16)
                        dve.wait_ge(stored[k], i * 16 + 16)
                        nc.vector.tensor_tensor(h[k][:], o_ps[k][:], x[k][:], ALU.add).then_inc(added, 1)


def memory_kv(nc, c, mem, gain, w_fm, w_v, km, vm):
    with Scope(nc) as sc:
        memT = sc.sb("memT", [P, D // P, MEM])
        norm_rows(nc, c, mem, gain, MEM, D, dstT=memT)
        project(nc, memT, D // P, MEM, w_fm, 2, c.fm_one, km, [(w_v, vm, 2 * P, False)])


def token_view(d, col, w):
    return d.rearrange("(t p) n -> p t n", p=P)[:, :, bass.ds(col, w)]


def memory_attention(nc, c, fm, km, vm, gm, y, ycol):
    def loads(i, j):
        pair = i * 2 + j
        return (fm[bass.ds((pair + FM0["qm"]) * P, P), :], [km[bass.ds(pair * P, P), :]],
                token_view(vm, pair * P, P), token_view(gm, pair * P, P))

    softmax_attention(nc, c, 1, [(b, [0, 1]) for b in range(NT)], loads, MEM,
                      lambda i, j: token_view(y, (i * 2 + j) * P + ycol, P), c.scale_m, None,
                      lambda u: c.zero_bias[:])


def trunk(nc, a, out):
    def dram(name, shape):
        return nc.dram_tensor(name, shape, F32, kind="Internal").ap()

    x, mem = a["x"][0], a["mem"][0]
    fm0, fm1 = dram("fm0", (NFM * P, S)), dram("fm1", (NFM * P, S))
    va, ga = dram("va", (S, P)), dram("ga", (S, A_HEADS * HD))
    vb, gb = dram("vb", (S, B_HEADS * HD)), dram("gb", (S, B_HEADS * HD))
    gm0, gm1 = dram("gm0", (S, M_HEADS * HD)), dram("gm1", (S, M_HEADS * HD))
    km0, km1, vm0, vm1 = (dram(n, (MEM, MEM)) for n in ("km0", "km1", "vm0", "vm1"))
    y0, y1 = dram("y0", (S, YW)), dram("y1", (S, YW))
    h1, h2 = dram("h1", (S, D)), dram("h2", (S, D))
    ckv, wi, gc = dram("ckv", (S, LAT)), dram("wi", (S, I_HEADS)), dram("gc", (S, C_HEADS * HD))
    kc, vc = dram("kc", (C_HEADS * HD, S)), dram("vc", (S, C_HEADS * HD))

    with Scope(nc) as top:
        c = make_constants(nc, top, a["e_sinks"])

        memory_kv(nc, c, mem, a["e_mem_norm"], a["e_mem_k"], a["e_w_mem_kv"][0][:, MEM:2 * MEM], km0, vm0)
        memory_kv(nc, c, mem, a["o_mem_norm"], a["o_mem_k"], a["o_w_mem_kv"][0][:, MEM:2 * MEM], km1, vm1)
        with Scope(nc) as sc:
            hT = sc.sb("hT", [P, D // P, S])
            norm_rows(nc, c, x, a["e_norm"], S, D, dstT=hT)
            w = a["e_w_in"][0]
            project(nc, hT, D // P, S, a["e_fm"], NFM, c.fm_scale0, fm0,
                    [(w[:, 640:768], va, 128, False), (w[:, 768:1280], ga, 512, True),
                     (w[:, 2304:2816], vb, 512, False), (w[:, 2816:3328], gb, 512, True),
                     (w[:, 3584:3840], gm0, 256, True)])

        def loads_a(i, j):
            return (fm0[bass.ds((i * 2 + j + FM0["qa"]) * P, P), :],
                    [fm0[bass.ds(i * HD + FM0["ka"] * P, HD), :] for _ in range(2)],
                    token_view(va, i * HD, HD), token_view(ga, (i * 2 + j) * P, P))

        softmax_attention(nc, c, 2, [(b, list(range(max(b - 1, 0), b + 1))) for b in range(NT)], loads_a, S,
                          lambda i, j: token_view(y0, (i * 2 + j) * P, P), c.slope_a, c.sink,
                          lambda u: c.window[:, 0 if u.b else P:2 * P], v_shared=True)
        stick_breaking(nc, c, fm0, vb, gb, y0)
        memory_attention(nc, c, fm0, km0, vm0, gm0, y0, (A_HEADS + B_HEADS) * HD)
        out_project(nc, c, y0, a["e_w_out"][0], x, h1)

        with Scope(nc) as sc:
            hT = sc.sb("hT", [P, D // P, S])
            norm_rows(nc, c, h1, a["o_norm"], S, D, dstT=hT)
            w = a["o_w_in"][0]
            project(nc, hT, D // P, S, a["o_fm"], NFM, c.fm_scale1, fm1,
                    [(w[:, 1024:1280], ckv, 256, False), (w[:, 1856:1864], wi, 8, False),
                     (w[:, 1864:2376], gc[:, 0:512], 512, True), (w[:, 2376:2888], gc[:, 512:1024], 512, True),
                     (w[:, 3144:3400], gm1, 256, True)])
        with Scope(nc) as sc:
            cT = sc.sb("cT", [P, LAT // P, S])
            norm_rows(nc, c, ckv, a["o_kv_norm"], S, LAT, dstT=cT)
            uv = a["o_w_uv"][0].rearrange("l h d -> l (h d)")
            project(nc, cT, LAT // P, S, a["o_uk"], 8, c.fm_one, kc,
                    [(uv[:, 0:512], vc[:, 0:512], 512, False), (uv[:, 512:1024], vc[:, 512:1024], 512, False)])
        memory_attention(nc, c, fm1, km1, vm1, gm1, y1, C_HEADS * HD)
        with Scope(nc) as sc:
            all_scores = sc.sb("scores", [P, P * (NT * (NT + 1) // 2)])

            def scores(b):
                o = P * (b * (b + 1) // 2)
                return all_scores[:, o:o + (b + 1) * P]

            index_scores(nc, c, fm1, wi, scores)
            select_keys(nc, c, scores, all_scores)

            def loads_c(i, j):
                pair = i * 2 + j
                return (fm1[bass.ds((pair + FM1["qc"]) * P, P), :], [kc[bass.ds(pair * P, P), :]],
                        token_view(vc, pair * P, P), token_view(gc, pair * P, P))

            softmax_attention(nc, c, C_HEADS // 4, [(b, list(range(b + 1))) for b in range(NT)], loads_c, S,
                              lambda i, j: token_view(y1, (i * 2 + j) * P, P), c.slope_c, None,
                              lambda u: scores(u.b))
        out_project(nc, c, y1, a["o_w_out"][0], h1, h2)
        norm_rows(nc, c, h2, a["final_norm"].rearrange("(a n) -> a n", a=1), S, D, out=out[0])


def tiles(w, starts):
    import numpy as np
    return np.ascontiguousarray(np.stack([w[:, s:s + P].reshape(-1, P, P).transpose(1, 0, 2) for s in starts]))


def kernel(**inputs):
    import numpy as _np
    import concourse.bacc as _bacc
    from concourse import mybir as _mybir
    from concourse.bass_utils import run_bass_kernel_spmd as _run

    nc = _bacc.Bacc("TRN2", target_bir_lowering=False, num_devices=1)
    arrays = {k: _np.ascontiguousarray(v) for k, v in inputs.items()}
    e, o = arrays["e_w_in"][0], arrays["o_w_in"][0]
    arrays["e_fm"] = tiles(e, [0, 128, 256, 384, 512] + list(range(1280, 2304, 128)) + [3328, 3456])
    arrays["o_fm"] = tiles(o, list(range(0, 1024, 128)) + list(range(1280, 1793, 128)) + [2888, 3016])
    arrays["e_mem_k"] = tiles(arrays["e_w_mem_kv"][0], [0, 128])
    arrays["o_mem_k"] = tiles(arrays["o_w_mem_kv"][0], [0, 128])
    arrays["o_uk"] = tiles(arrays.pop("o_w_uk")[0].reshape(LAT, C_HEADS * HD), list(range(0, 1024, 128)))
    aps = {k: nc.dram_tensor("in_" + k, v.shape, _mybir.dt.from_np(v.dtype), kind="ExternalInput").ap()
           for k, v in arrays.items()}
    out = nc.dram_tensor("out_0", (1, S, D), _mybir.dt.float32, kind="ExternalOutput").ap()
    trunk(nc, aps, out)
    r = _run(nc, [{"in_" + k: v for k, v in arrays.items()}], core_ids=[0])
    return r.results[0]["out_0"]
```

```python
from contextlib import ExitStack

import concourse.bass as bass
from concourse import mybir

F32 = mybir.dt.float32
BF16 = mybir.dt.bfloat16
I32 = mybir.dt.int32
U32 = mybir.dt.uint32
ALU = mybir.AluOpType
ACT = mybir.ActivationFunctionType
AX_X = mybir.AxisListType.X

P = 128
S = 2048
D = 1024
NT = S // P
HD = 64
EPS = 1e-6
MEM = 256
TOPK = 256
LAT = 256
A_HEADS, B_HEADS, C_HEADS, I_HEADS, M_HEADS = 8, 8, 16, 8, 4
SCALE = HD ** -0.5
IDX_SCALE = (HD ** -0.5) * (I_HEADS ** -0.5)
MASKED = -1.0e30
NEVER = -3.0e38
YW = 1280
BANK = 512
SIGN = 0x80000000
PIECE = 1024
PB = PIECE // P
GB = BANK // P

FM0 = {"qa": 0, "ka": 4, "qb": 5, "kb": 9, "qm": 13}
FM1 = {"qc": 0, "qi": 8, "ki": 12, "qm": 13}
NFM = 15


def slopes(n):
    return [2.0 ** (-8.0 * h / n) for h in range(1, n + 1)]


def chunks(n, w):
    return [(a, min(w, n - a)) for a in range(0, n, w)]


class Scope:

    made = 0

    def __init__(self, nc):
        self.nc = nc
        self.ctx = ExitStack()
        Scope.made += 1
        self.tag = f"s{Scope.made}_"
        self.taken = []

    def __enter__(self):
        return self

    def __exit__(self, *e):
        if self.taken and e[0] is None:
            with self.nc.Block() as block:
                @block.sync
                def _(sp):
                    for s in self.taken:
                        sp.sem_clear(s)
        self.ctx.close()

    def sb(self, name, shape, dt=F32):
        return self.ctx.enter_context(self.nc.sbuf_tensor(self.tag + name, shape, dt))

    def ps(self, name, shape, dt=F32):
        return self.ctx.enter_context(self.nc.psum_tensor(self.tag + name, shape, dt))

    def sem(self, name):
        self.taken.append(self.ctx.enter_context(self.nc.semaphore(self.tag + name)))
        return self.taken[-1]

    def sems(self, name, n):
        return [self.sem(f"{name}{k}") for k in range(n)]


class Constants:
    pass


def make_constants(nc, sc, e_sinks):
    c = Constants()
    c.ident = sc.sb("ident", [P, P])
    c.identb = sc.sb("identb", [P, P], BF16)
    c.neg_dist = sc.sb("neg_dist", [P, S])
    c.causal = sc.sb("causal", [P, P], BF16)
    c.window = sc.sb("window", [P, 2 * P])
    c.zero_bias = sc.sb("zero_bias", [P, MEM])
    c.slope_a = sc.sb("slope_a", [P, A_HEADS])
    c.slope_c = sc.sb("slope_c", [P, C_HEADS])
    c.scale_m = sc.sb("scale_m", [P, M_HEADS])
    c.fm_scale0 = sc.sb("fm_scale0", [P, 16])
    c.fm_scale1 = sc.sb("fm_scale1", [P, 16])
    c.fm_one = sc.sb("fm_one", [P, 8])
    c.sink = sc.sb("sink", [P, A_HEADS])
    with Scope(nc) as st:
        ramp = st.sb("ramp", [P, S], I32)
        cleared = st.sem("cleared")
        ramp_made = st.sem("ramp_made")
        dist_made = st.sem("dist_made")
        sinks_in = st.sem("sinks_in")
        with nc.Block() as block:
            @block.gpsimd
            def _(pool):
                nc.gpsimd.iota(ramp[:], pattern=[[-1, S]], base=S - P, channel_multiplier=1).then_inc(ramp_made, 1)
                for t in (c.ident, c.identb, c.causal):
                    nc.gpsimd.memset(t[:], 0.0).then_inc(cleared, 1)
                pool.wait_ge(cleared, 3)
                for t in (c.ident, c.identb):
                    nc.gpsimd.affine_select(out=t[:], in_=t[:], compare_op=ALU.not_equal, fill=1.0, base=0,
                                            pattern=[[-1, P]], channel_multiplier=1)
                nc.gpsimd.affine_select(out=c.causal[:], in_=c.causal[:], compare_op=ALU.is_gt, fill=MASKED,
                                        base=0, pattern=[[-1, P]], channel_multiplier=1)

            @block.sync
            def _(sp):
                sp.dma_start(c.sink[:], e_sinks[0:1, :].broadcast_to([P, A_HEADS])).then_inc(sinks_in, 16)
                sp.wait_ge(sinks_in, 16)

            @block.vector
            def _(dve):
                v = nc.vector
                dve.wait_ge(ramp_made, 1)
                v.tensor_copy(c.neg_dist[:], ramp[:]).then_inc(dist_made, 1)
                dve.wait_ge(dist_made, 1)
                v.scalar_tensor_tensor(out=c.neg_dist[:], in0=c.neg_dist[:], scalar=-1.0, in1=c.neg_dist[:],
                                       op0=ALU.mult, op1=ALU.min).then_inc(dist_made, 1)
                dve.wait_ge(dist_made, 2)
                v.tensor_copy(c.window[:], c.neg_dist[:, S - 2 * P:S]).then_inc(dist_made, 1)
                dve.wait_ge(dist_made, 3)
                v.memset(c.window[0:64, 0:64], MASKED)
                v.memset(c.window[64:128, 0:128], MASKED)
                v.memset(c.window[0:64, 192:256], MASKED)
                v.memset(c.zero_bias[:], 0.0)
                for t, n in ((c.slope_a, A_HEADS), (c.slope_c, C_HEADS)):
                    for h, s in enumerate(slopes(n)):
                        v.memset(t[:, h:h + 1], s)
                v.memset(c.scale_m[:], SCALE)
                v.memset(c.fm_scale0[:, 4:16], 1.0)
                v.memset(c.fm_scale1[:, 8:16], 1.0)
                v.memset(c.fm_one[:], 1.0)
                for t, n in ((c.fm_scale0, A_HEADS), (c.fm_scale1, C_HEADS)):
                    for h, s in enumerate(slopes(n)):
                        v.memset(t[HD * (h % 2):HD * (h % 2) + HD, h // 2:h // 2 + 1], SCALE / s)
    return c


def norm_rows(nc, c, src, gain, T, W, dstT=None, out=None):
    nt, kt = T // P, W // P
    half = nt // 2
    with Scope(nc) as sc:
        x = sc.sb("x", [P, nt, W])
        g = sc.sb("g", [P, W])
        xn = sc.sb("xn", [P, 2, W])
        sq = sc.sb("sq", [P, 2, W])
        ss = sc.sb("ss", [P, nt])
        rms = sc.sb("rms", [P, nt])
        rstd = sc.sb("rstd", [P, nt])
        tp = [sc.ps(f"tp{k}", [P, max(W, BANK)]) for k in range(2)]
        x_in = sc.sems("x_in", 2)
        g_in = sc.sem("g_in")
        squared = sc.sem("squared")
        mean_made = sc.sem("mean_made")
        root_made = sc.sem("root_made")
        rstd_made = sc.sem("rstd_made")
        normed = sc.sem("normed")
        turned = sc.sem("turned")
        evacuated = sc.sem("evacuated")
        stored = sc.sems("stored", 2)
        xv = src.rearrange("(t p) d -> p t d", p=P)
        with nc.Block() as block:
            @block.sync
            def _(sp):
                for k in range(2):
                    sp.dma_start(x[:, k * half:(k + 1) * half, :], xv[:, k * half:(k + 1) * half, :]
                                 ).then_inc(x_in[k], 16)
                sp.dma_start(g[:], gain.broadcast_to([P, W])).then_inc(g_in, 16)
                if out is not None:
                    with sp.Fori(0, half) as i:
                        for k in range(2):
                            sp.wait_ge(normed, i * 2 + k + 1)
                            sp.dma_start(out[bass.ds((i * 2 + k) * P, P), :], xn[:, k, :]).then_inc(stored[k], 16)
                    for k in range(2):
                        sp.wait_ge(stored[k], 16 * (half + 1))

            @block.scalar
            def _(act):
                for t in range(nt):
                    if t % half == 0:
                        act.wait_ge(x_in[t // half], 16)
                    if t >= 2:
                        act.wait_ge(squared, t - 1)
                    nc.scalar.activation(sq[:, t % 2, :], x[:, t, :], ACT.Square, accum_out=ss[:, t:t + 1]
                                         ).then_inc(squared, 1)
                act.wait_ge(mean_made, 1)
                nc.scalar.activation(rms[:], rms[:], ACT.Sqrt).then_inc(root_made, 1)
                if dstT is not None:
                    with act.Fori(0, half) as i:
                        for k in range(2):
                            act.wait_ge(turned, i * 2 + k + 1 + 2)
                            nc.scalar.copy(dstT[:, :, bass.ds((i * 2 + k) * P, P)],
                                           tp[k][:, 0:W].rearrange("p (k t) -> p k t", k=kt)
                                           ).then_inc(evacuated, 1)

            @block.vector
            def _(dve):
                dve.wait_ge(squared, nt)
                nc.vector.tensor_scalar(rms[:], ss[:], 1.0 / W, EPS, ALU.mult, ALU.add).then_inc(mean_made, 1)
                dve.wait_ge(root_made, 1)
                nc.vector.reciprocal(rstd[:], rms[:]).then_inc(rstd_made, 1)
                dve.wait_ge(rstd_made, 1)
                dve.wait_ge(g_in, 16)
                for k in range(2):
                    dve.wait_ge(x_in[k], 16)
                if dstT is not None:
                    dve.sem_inc(turned, 2)
                else:
                    for k in range(2):
                        dve.sem_inc(stored[k], 16)
                with dve.Fori(0, half) as i:
                    for k in range(2):
                        if dstT is not None:
                            dve.wait_ge(turned, i * 2 + k + 1)
                        else:
                            dve.wait_ge(stored[k], i * 16 + 16)
                        nc.vector.scalar_tensor_tensor(
                            out=xn[:, k, :], in0=x[:, bass.ds(i * 2 + k, 1), :].rearrange("p a d -> p (a d)"),
                            scalar=rstd[:, bass.ds(i * 2 + k, 1)], in1=g[:], op0=ALU.mult, op1=ALU.mult
                        ).then_inc(normed, 1)

            if dstT is not None:
                @block.tensor
                def _(pe):
                    pe.sem_inc(evacuated, 2)
                    with pe.Fori(0, half) as i:
                        for k in range(2):
                            pe.wait_ge(normed, i * 2 + k + 1)
                            pe.wait_ge(evacuated, i * 2 + k + 1)
                            for j in range(kt):
                                last = nc.tensor.transpose(tp[k][:, j * P:(j + 1) * P], xn[:, k, j * P:(j + 1) * P],
                                                           c.ident[:])
                            last.then_inc(turned, 1)


def in_pairs(eng, n, body):
    if n // 2 > 1:
        with eng.Fori(0, n // 2) as i:
            for k in range(2):
                body(i, k)
    elif n // 2 == 1:
        for k in range(2):
            body(0, k)
    if n % 2:
        body(n // 2, 0)


def project(nc, srcT, KT, T, w_fm, nfm, fm_scale, fm_out, tm_jobs):
    gw = min(BANK, T)
    ng = T // gw
    nt = T // P
    TG = min(4, nt)
    with Scope(nc) as sc:
        w = [sc.sb(f"w{k}", [P, KT, BANK]) for k in range(2)]
        stage = [sc.sb(f"stage{k}", [P, T]) for k in range(2)]
        scale = sc.sb("scale", [P, 2])
        rows = [sc.sb(f"rows{k}", [P, TG, BANK]) for k in range(2)]
        sig = [sc.sb(f"sig{k}", [P, BANK]) for k in range(2)]
        acc = [sc.ps(f"acc{k}", [P, BANK]) for k in range(4)]
        w_in = sc.sems("w_in", 2)
        scale_set = sc.sem("scale_set")
        summed = sc.sem("summed")
        staged = sc.sem("staged")
        stored = sc.sems("stored", 2)
        sig_made = sc.sem("sig_made")
        rowed = sc.sem("rowed")
        rows_out = sc.sems("rows_out", 2)
        nrow = nt * len(tm_jobs)
        nquad = nrow // TG
        with nc.Block() as block:
            @block.sync
            def _(sp):
                def load_fm(n, k):
                    sp.dma_start(w[k][:, :, 0:P], w_fm[bass.ds(n, 1), :, :, :].rearrange("a p k m -> p (a k) m")
                                 ).then_inc(w_in[k], 16)

                for n in range(min(2, nfm)):
                    load_fm(n, n)

                def step(i, k):
                    sp.wait_ge(summed, (i * 2 + k) * ng + ng)
                    load_fm(i * 2 + k + 2, k)

                in_pairs(sp, nfm - 2, step)
                for n, (wd, _, width, _) in enumerate(tm_jobs):
                    m = nfm + n
                    sp.wait_ge(summed, ng * (m - 1) if m - 2 < nfm else ng * nfm + nt * (m - 1 - nfm))
                    sp.dma_start(w[m % 2][:, :, 0:width], wd.rearrange("(k p) n -> p k n", p=P)
                                 ).then_inc(w_in[m % 2], 16)

            @block.tensor
            def _(pe):
                pe.sem_inc(staged, ng)
                pe.sem_inc(rowed, 4)

                def step(i, k):
                    pe.wait_ge(w_in[k], i * 16 + 16)
                    for g in range(ng):
                        pe.wait_ge(staged, (i * 2 + k) * ng + g + 1)
                        for j in range(KT):
                            last = nc.tensor.matmul(acc[g][:, 0:gw], w[k][:, j, 0:P], srcT[:, j, g * gw:(g + 1) * gw],
                                                    start=(j == 0), stop=(j == KT - 1))
                        last.then_inc(summed, 1)

                in_pairs(pe, nfm, step)
                pe.wait_ge(staged, ng * nfm + ng)
                for n, (_, _, width, _) in enumerate(tm_jobs):
                    m = nfm + n
                    pe.wait_ge(w_in[m % 2], 16 * (m // 2 + 1))
                    for t in range(nt):
                        r = n * nt + t
                        pe.wait_ge(rowed, r + 1)
                        for j in range(KT):
                            last = nc.tensor.matmul(acc[r % 4][:, 0:width], srcT[:, j, t * P:(t + 1) * P],
                                                    w[m % 2][:, j, 0:width], start=(j == 0), stop=(j == KT - 1))
                        last.then_inc(summed, 1)

            @block.scalar
            def _(act):
                for k in range(2):
                    act.sem_inc(stored[k], 16)
                    act.sem_inc(rows_out[k], 16)

                def step(i, k):
                    act.wait_ge(stored[k], i * 16 + 16)
                    nc.scalar.copy(scale[:, k:k + 1], fm_scale[:, bass.ds(i * 2 + k, 1)]).then_inc(scale_set, 1)
                    act.wait_ge(scale_set, i * 2 + k + 1)
                    for g in range(ng):
                        act.wait_ge(summed, (i * 2 + k) * ng + g + 1)
                        nc.scalar.mul(stage[k][:, g * gw:(g + 1) * gw], acc[g][:, 0:gw],
                                      scale[:, k:k + 1]).then_inc(staged, 1)
                    act.wait_ge(staged, (i * 2 + k) * ng + 2 * ng)
                    act.dma_start(fm_out[bass.ds((i * 2 + k) * P, P), :], stage[k][:, :]).then_inc(stored[k], 16)

                in_pairs(act, nfm, step)
                for n, (_, od, width, silu) in enumerate(tm_jobs):
                    for t in range(nt):
                        r = n * nt + t
                        if silu:
                            act.wait_ge(summed, ng * nfm + r + 1)
                            act.wait_ge(rowed, r + 3)
                            nc.scalar.activation(sig[r % 2][:, 0:width], acc[r % 4][:, 0:width], ACT.Sigmoid
                                                 ).then_inc(sig_made, 1)
                        if r % TG == TG - 1:
                            q = r // TG
                            act.wait_ge(rowed, r + 5)
                            act.dma_start(od[(t - TG + 1) * P:(t + 1) * P, :].rearrange("(t p) n -> p t n", p=P),
                                          rows[q % 2][:, :, 0:width]).then_inc(rows_out[q % 2], 16)
                for k in range(2):
                    act.wait_ge(stored[k], 16 * ((nfm + 1 - k) // 2 + 1))
                    act.wait_ge(rows_out[k], 16 * ((nquad + 1 - k) // 2 + 1))

            @block.vector
            def _(dve):
                gates = 0
                for n, (_, _, width, silu) in enumerate(tm_jobs):
                    for t in range(nt):
                        r = n * nt + t
                        q = r // TG
                        if r % TG == 0:
                            if q == 0:
                                dve.wait_ge(summed, ng * nfm + 1)
                            dve.wait_ge(rows_out[q % 2], 16 * (q // 2 + 1))
                        dve.wait_ge(summed, ng * nfm + r + 1)
                        dst = rows[q % 2][:, r % TG, 0:width]
                        if silu:
                            gates += 1
                            dve.wait_ge(sig_made, gates)
                            nc.vector.tensor_tensor(dst, acc[r % 4][:, 0:width], sig[r % 2][:, 0:width], ALU.mult
                                                    ).then_inc(rowed, 1)
                        else:
                            nc.vector.tensor_copy(dst, acc[r % 4][:, 0:width]).then_inc(rowed, 1)


class Unit:

    def __init__(self, j, hh, b, kbs):
        self.j, self.hh, self.b, self.kbs = j, hh, b, kbs


class Group:

    def __init__(self, ui, u, a, m, first, last):
        self.ui, self.u, self.a, self.m, self.first, self.last = ui, u, a, m, first, last


def groups_of(units, latest_first=False):
    out = []
    for ui, u in enumerate(units):
        parts = chunks(len(u.kbs), GB)
        u.first, u.ng = len(out), len(parts)
        for n, (a, m) in enumerate(reversed(parts) if latest_first else parts):
            out.append(Group(ui, u, a, m, n == 0, n == len(parts) - 1))
    return out


def shares(n, of_vector):
    who = ["v" if of_vector(k) else "s" for k in range(n)]
    return who, [who[:k + 1].count(who[k]) for k in range(n)], {w: who.count(w) for w in "vs"}


def transpose_group(nc, c, t_ps, probs, g, turned):
    for x in range(g.m):
        last = nc.tensor.transpose(t_ps[:, x * P:(x + 1) * P], probs[:, x * P:(x + 1) * P], c.ident[:])
    last.then_inc(turned, 1)


def values_group(nc, o_ps, pT, v, g, vc, fed):
    for x in range(g.m):
        for r in range(0, P, HD):
            last = nc.tensor.matmul(o_ps[r:r + HD, 0:HD], pT[:, x * P + r:x * P + r + HD],
                                    v[:, g.u.kbs[g.a + x], vc:vc + HD],
                                    start=(g.first and x == 0), stop=(g.last and x == g.m - 1),
                                    skip_group_check=True)
    last.then_inc(fed, 1)


def softmax_attention(nc, c, steps, per_pair, loads, NK, y_out, scale_tab, sink, bias_of, v_shared=False):
    units = [Unit(j, hh, b, kbs) for j in range(2) for b, kbs in per_pair for hh in range(2)]
    gs = groups_of(units)
    NG, NU, LEAD, EXP_LEAD, R, US = len(gs), len(units), 7, 2, 8, 16
    assert NG % R == 0 and NU % US == 0
    who, nth, per_step = shares(NG, lambda k: k % 4 == 3)
    VW = HD if v_shared else 2 * HD
    with Scope(nc) as sc:
        q = [sc.sb(f"q{k}", [P, S]) for k in range(2)]
        kk = [sc.sb(f"k{k}", [P, NK]) for k in range(2)]
        v = [sc.sb(f"v{k}", [P, NK // P, VW]) for k in range(2)]
        gt = [sc.sb(f"g{k}", [P, NT, 2 * HD]) for k in range(2)]
        y = [sc.sb(f"y{k}", [P, NT, 2 * HD]) for k in range(2)]
        probs = [sc.sb(f"probs{k}", [P, BANK]) for k in range(R)]
        pT = [sc.sb(f"pT{k}", [P, BANK]) for k in range(4)]
        mx = sc.sb("mx", [P, US, 4])
        top = sc.sb("top", [P, US, 2])
        nmx = sc.sb("nmx", [P, US])
        rsum = sc.sb("rsum", [P, US, 4])
        esink = sc.sb("esink", [P, US])
        den = sc.sb("den", [P, US, 2])
        rden = sc.sb("rden", [P, US])
        gate = sc.sb("gate", [P, US])
        scales = sc.sb("scales", [P, 4])
        sinks = sc.sb("sinks", [P, 4])
        s_ps = [sc.ps(f"s{k}", [P, BANK]) for k in range(4)]
        t_ps = [sc.ps(f"t{k}", [P, BANK]) for k in range(2)]
        o_ps = [sc.ps(f"o{k}", [P, BANK]) for k in range(2)]
        heads_set = sc.sem("heads_set")
        loaded = sc.sems("loaded", 2)
        pair_done = sc.sem("pair_done")
        y_stored = sc.sems("y_stored", 2)
        scored = sc.sem("scored")
        biased = sc.sem("biased")
        chain = sc.sem("chain")
        max_made = sc.sem("max_made")
        exp_made = sc.sem("exp_made")
        turned = sc.sem("turned")
        taken = {"s": sc.sem("taken_s"), "v": sc.sem("taken_v")}
        fed = sc.sem("fed")
        out_made = sc.sem("out_made")
        nload = 5 if v_shared else 4
        links = sum((u.ng > 1) + (sink is not None) + (u.ng > 1) + (sink is not None) + 1 for u in units)

        with nc.Block() as block:
            @block.sync
            def _(sp):
                sp.sem_inc(pair_done, 2)
                with sp.Fori(0, steps) as i:
                    for j in range(2):
                        sp.wait_ge(pair_done, i * 2 + j + 1)
                        qd, kds, vd, gd = loads(i, j)
                        sp.dma_start(q[j][:], qd).then_inc(loaded[j], 16)
                        w = P // len(kds)
                        for n, kd in enumerate(kds):
                            sp.dma_start(kk[j][n * w:(n + 1) * w, :], kd).then_inc(loaded[j], 16)
                        sp.dma_start(v[j][:], vd).then_inc(loaded[j], 16)
                        sp.dma_start(gt[j][:], gd).then_inc(loaded[j], 16)

            @block.tensor
            def _(pe):
                pe.sem_inc(biased, 4)
                pe.sem_inc(taken["s"], 1)
                pe.sem_inc(taken["v"], 1)
                pe.sem_inc(out_made, 2)

                def score(i, k):
                    g = gs[k]
                    u = g.u
                    r = slice(HD * u.hh, HD * u.hh + HD)
                    if g.first:
                        pe.wait_ge(loaded[u.j], i * (16 * nload) + 16 * nload)
                    pe.wait_ge(biased, i * NG + k + 1)
                    k0 = (u.kbs[0] + g.a) * P
                    nc.tensor.matmul(s_ps[k % 4][:, 0:g.m * P], q[u.j][r, u.b * P:(u.b + 1) * P],
                                     kk[u.j][r, k0:k0 + g.m * P], start=True, stop=True).then_inc(scored, 1)

                def turn(i, n):
                    pe.wait_ge(exp_made, i * NG + n + 1)
                    w = who[n - 2]
                    pe.wait_ge(taken[w], i * per_step[w] + (nth[n - 2] if n >= 2 else 0) + 1)
                    transpose_group(nc, c, t_ps[n % 2], probs[n % R], gs[n], turned)

                def feed(i, n):
                    g = gs[n]
                    if g.first:
                        pe.wait_ge(out_made, i * NU + g.ui + 1)
                    pe.wait_ge(taken[who[n]], i * per_step[who[n]] + nth[n] + 1)
                    values_group(nc, o_ps[g.ui % 2], pT[n % 4], v[g.u.j], g, 0 if v_shared else HD * g.u.hh, fed)

                with pe.Fori(0, steps) as i:
                    for k in range(LEAD):
                        score(i, k)
                    for n in range(NG):
                        turn(i, n)
                        if n + LEAD < NG:
                            score(i, n + LEAD)
                        if n:
                            feed(i, n - 1)
                    feed(i, NG - 1)

            def copy_out(eng, copy, i, n):
                eng.wait_ge(fed, i * NG + n + 1)
                eng.wait_ge(turned, i * NG + n + 1 + R)
                copy(pT[n % 4][:, 0:gs[n].m * P], t_ps[n % 2][:, 0:gs[n].m * P]).then_inc(taken[who[n]], 1)

            @block.scalar
            def _(act):
                act.sem_inc(fed, 4)

                def exponential(i, k):
                    g = gs[k]
                    u, us = g.u, g.ui % US
                    h4 = u.j * 2 + u.hh
                    if g.first:
                        act.wait_ge(max_made, i * NU + g.ui + 1)
                        if sink is not None:
                            nc.scalar.activation(esink[:, us:us + 1], sinks[:, h4:h4 + 1], ACT.Exp,
                                                 bias=nmx[:, us:us + 1])
                    e = probs[k % R][:, 0:g.m * P]
                    part = k - u.first
                    nc.scalar.activation(e, e, ACT.Exp, bias=nmx[:, us:us + 1], scale=scales[:, h4:h4 + 1],
                                         accum_out=rsum[:, us, part:part + 1]).then_inc(exp_made, 1)

                with act.Fori(0, steps) as i:
                    act.wait_ge(heads_set, i + 1)
                    for k in range(EXP_LEAD):
                        exponential(i, k)
                    for n in range(NG):
                        if n + EXP_LEAD < NG:
                            exponential(i, n + EXP_LEAD)
                        if who[n] == "s":
                            copy_out(act, nc.scalar.copy, i, n)
                        if n in (NG // 2 + 4, NG - 1):
                            j = n // (NG // 2 + 5)
                            act.wait_ge(pair_done, i * 2 + j + 3)
                            act.dma_start(y_out(i, j), y[j][:]).then_inc(y_stored[j], 16)
                for j in range(2):
                    act.wait_ge(y_stored[j], 16 * (steps + 1))

            @block.vector
            def _(dve):
                dve.sem_inc(turned, R)
                for j in range(2):
                    dve.sem_inc(y_stored[j], 16)

                with dve.Fori(0, steps) as i:
                    done = [0]

                    def link(ins):
                        done[0] += 1
                        ins.then_inc(chain, 1)
                        dve.wait_ge(chain, i * links + done[0])

                    def bias(k):
                        g = gs[k]
                        u, us = g.u, g.ui % US
                        part = k - u.first
                        dve.wait_ge(turned, i * NG + k + 1)
                        dve.wait_ge(scored, i * NG + k + 1)
                        nc.vector.memset(gate[:, k % US:k % US + 1], 0.0)
                        nc.vector.tensor_tensor_reduce(
                            out=probs[k % R][:, 0:g.m * P], in0=s_ps[k % 4][:, 0:g.m * P],
                            in1=bias_of(u)[:, g.a * P:(g.a + g.m) * P], scale=1.0, scalar=NEVER, op0=ALU.add,
                            op1=ALU.max, accum_out=mx[:, us, part:part + 1]).then_inc(biased, 1)
                        if not g.last:
                            return
                        dve.wait_ge(biased, i * NG + k + 5)
                        m0 = mx[:, us, 0:1]
                        if u.ng > 1:
                            m0 = top[:, us, 0:1]
                            link(nc.vector.tensor_reduce(m0, mx[:, us, 0:u.ng], AX_X, ALU.max))
                        scl = scales[:, u.j * 2 + u.hh:u.j * 2 + u.hh + 1]
                        if sink is not None:
                            link(nc.vector.tensor_scalar(top[:, us, 1:2], m0, scl,
                                                         sinks[:, u.j * 2 + u.hh:u.j * 2 + u.hh + 1],
                                                         ALU.mult, ALU.max))
                            nc.vector.tensor_scalar(nmx[:, us:us + 1], top[:, us, 1:2], -1.0, None,
                                                    ALU.mult).then_inc(max_made, 1)
                        else:
                            nc.vector.tensor_scalar(nmx[:, us:us + 1], m0, scl, -1.0, ALU.mult, ALU.mult
                                                    ).then_inc(max_made, 1)

                    def output(ui):
                        u, us = units[ui], ui % US
                        last = u.first + u.ng - 1
                        dve.wait_ge(exp_made, i * NG + last + 1)
                        d = rsum[:, us, 0:1]
                        if u.ng > 1:
                            d = den[:, us, 0:1]
                            link(nc.vector.reduce_sum(d, rsum[:, us, 0:u.ng], AX_X))
                        if sink is not None:
                            link(nc.vector.tensor_tensor(den[:, us, 1:2], d, esink[:, us:us + 1], ALU.add))
                            d = den[:, us, 1:2]
                        link(nc.vector.reciprocal(rden[:, us:us + 1], d))
                        if ui % (NU // 2) == 0:
                            dve.wait_ge(y_stored[u.j], i * 16 + 16)
                            dve.wait_ge(loaded[u.j], i * (16 * nload) + 16 * nload)
                        dve.wait_ge(fed, i * NG + last + 5)
                        cc = slice(HD * u.hh, HD * u.hh + HD)
                        nc.vector.scalar_tensor_tensor(
                            out=y[u.j][:, u.b, cc], in0=o_ps[ui % 2][:, 0:HD], scalar=rden[:, us:us + 1],
                            in1=gt[u.j][:, u.b, cc], op0=ALU.mult, op1=ALU.mult).then_inc(out_made, 1)
                        if ui % (NU // 2) == NU // 2 - 1:
                            dve.wait_ge(out_made, i * NU + ui + 3)
                            dve.sem_inc(pair_done, 1)

                    if sink is not None:
                        nc.vector.tensor_copy(sinks[:], sink[:, bass.ds(i * 4, 4)])
                    nc.vector.tensor_copy(scales[:], scale_tab[:, bass.ds(i * 4, 4)]).then_inc(heads_set, 1)
                    dve.wait_ge(heads_set, i + 1)
                    for k in range(LEAD):
                        bias(k)
                    for n in range(NG + 2):
                        if n + LEAD < NG:
                            bias(n + LEAD)
                        if n < NG and who[n] == "v":
                            copy_out(dve, nc.vector.tensor_copy, i, n)
                        if n >= 2 and gs[n - 2].last:
                            output(gs[n - 2].ui)
                    assert done[0] == links


def stick_breaking(nc, c, fm, vals, gates, y_dram):
    steps = B_HEADS // 4
    units = [Unit(j, hh, b, list(range(b + 1))) for j in range(2) for b in range(NT) for hh in range(2)]
    gs = groups_of(units, latest_first=True)
    NG, NU, LEAD, R = len(gs), len(units), 6, 8
    assert NG % R == 0 and NU % 2 == 0
    who, nth, per_step = shares(NG, lambda k: k % 2 == 1)
    with Scope(nc) as sc:
        q = [sc.sb(f"q{k}", [P, S]) for k in range(2)]
        kk = [sc.sb(f"k{k}", [P, S]) for k in range(2)]
        v = [sc.sb(f"v{k}", [P, NT, 2 * HD]) for k in range(2)]
        gt = [sc.sb(f"g{k}", [P, NT, 2 * HD]) for k in range(2)]
        y = [sc.sb(f"y{k}", [P, NT, 2 * HD]) for k in range(2)]
        beta = [sc.sb(f"beta{k}", [P, BANK]) for k in range(R)]
        keep = [sc.sb(f"keep{k}", [P, BANK]) for k in range(R)]
        left = [sc.sb(f"left{k}", [P, BANK + 8]) for k in range(R)]
        pT = [sc.sb(f"pT{k}", [P, BANK]) for k in range(4)]
        z_ps = [sc.ps(f"z{k}", [P, BANK]) for k in range(4)]
        t_ps = [sc.ps(f"t{k}", [P, BANK]) for k in range(2)]
        o_ps = [sc.ps(f"o{k}", [P, BANK]) for k in range(2)]
        loaded = sc.sems("loaded", 2)
        pair_done = sc.sem("pair_done")
        y_stored = sc.sems("y_stored", 2)
        scored = sc.sem("scored")
        squashed = sc.sem("squashed")
        edge = sc.sem("edge")
        scanned = sc.sem("scanned")
        weighed = sc.sem("weighed")
        turned = sc.sem("turned")
        taken = {"s": sc.sem("taken_s"), "v": sc.sem("taken_v")}
        fed = sc.sem("fed")
        out_made = sc.sem("out_made")

        with nc.Block() as block:
            @block.sync
            def _(sp):
                sp.sem_inc(pair_done, 2)
                with sp.Fori(0, steps) as i:
                    for j in range(2):
                        pair = i * 2 + j
                        sp.wait_ge(pair_done, pair + 1)
                        sp.dma_start(q[j][:], fm[bass.ds((pair + FM0["qb"]) * P, P), :]).then_inc(loaded[j], 16)
                        sp.dma_start(kk[j][:], fm[bass.ds((pair + FM0["kb"]) * P, P), :]).then_inc(loaded[j], 16)
                        for t, d in ((v[j], vals), (gt[j], gates)):
                            sp.dma_start(t[:], token_view(d, pair * P, P)).then_inc(loaded[j], 16)

            @block.tensor
            def _(pe):
                pe.sem_inc(squashed, 4)
                pe.sem_inc(taken["s"], 1)
                pe.sem_inc(taken["v"], 1)
                pe.sem_inc(out_made, 2)

                def score(i, k):
                    g = gs[k]
                    u, w = g.u, g.m * P
                    r = slice(HD * u.hh, HD * u.hh + HD)
                    if g.first:
                        pe.wait_ge(loaded[u.j], i * 64 + 64)
                    pe.wait_ge(squashed, i * NG + k + 1)
                    ins = nc.tensor.matmul(z_ps[k % 4][:, 0:w], q[u.j][r, u.b * P:(u.b + 1) * P],
                                           kk[u.j][r, g.a * P:g.a * P + w], start=True, stop=not g.first)
                    if g.first:
                        ins = nc.tensor.matmul(z_ps[k % 4][:, w - P:w], c.identb[:], c.causal[:],
                                               start=False, stop=True)
                    ins.then_inc(scored, 1)

                def turn(i, n):
                    pe.wait_ge(weighed, i * NG + n + 1 + R)
                    w = who[n - 2]
                    pe.wait_ge(taken[w], i * per_step[w] + (nth[n - 2] if n >= 2 else 0) + 1)
                    transpose_group(nc, c, t_ps[n % 2], beta[n % R], gs[n], turned)

                def feed(i, n):
                    g = gs[n]
                    if g.first:
                        pe.wait_ge(out_made, i * NU + g.ui + 1)
                    pe.wait_ge(taken[who[n]], i * per_step[who[n]] + nth[n] + 1)
                    values_group(nc, o_ps[g.ui % 2], pT[n % 4], v[g.u.j], g, HD * g.u.hh, fed)

                with pe.Fori(0, steps) as i:
                    for k in range(LEAD):
                        score(i, k)
                    for n in range(NG):
                        turn(i, n)
                        if n + LEAD < NG:
                            score(i, n + LEAD)
                        if n:
                            feed(i, n - 1)
                    feed(i, NG - 1)

            def copy_out(eng, copy, i, n):
                eng.wait_ge(fed, i * NG + n + 1)
                eng.wait_ge(turned, i * NG + n + 1 + R)
                copy(pT[n % 4][:, 0:gs[n].m * P], t_ps[n % 2][:, 0:gs[n].m * P]).then_inc(taken[who[n]], 1)

            @block.scalar
            def _(act):
                act.sem_inc(fed, 4)

                def squash(i, k):
                    w = gs[k].m * P
                    act.wait_ge(turned, i * NG + k + 1)
                    act.wait_ge(scored, i * NG + k + 1)
                    nc.scalar.activation(keep[k % R][:, 0:w], z_ps[k % 4][:, 0:w], ACT.Sigmoid, scale=-SCALE)
                    nc.scalar.activation(beta[k % R][:, 0:w], z_ps[k % 4][:, 0:w], ACT.Sigmoid, scale=SCALE
                                         ).then_inc(squashed, 1)

                with act.Fori(0, steps) as i:
                    for k in range(LEAD):
                        squash(i, k)
                    for n in range(NG):
                        if n + LEAD < NG:
                            squash(i, n + LEAD)
                        if who[n] == "s":
                            copy_out(act, nc.scalar.copy, i, n)
                        if n in (NG // 2 + 4, NG - 1):
                            j = n // (NG // 2 + 5)
                            act.wait_ge(pair_done, i * 2 + j + 3)
                            act.dma_start(token_view(y_dram, (i * 2 + j) * P + A_HEADS * HD, P), y[j][:]
                                          ).then_inc(y_stored[j], 16)
                for j in range(2):
                    act.wait_ge(y_stored[j], 16 * (steps + 1))

            @block.gpsimd
            def _(pool):
                with pool.Fori(0, steps) as i:
                    for k, g in enumerate(gs):
                        w = g.m * P
                        pool.wait_ge(scanned, i * NG + k + 1)
                        nc.gpsimd.tensor_tensor(beta[k % R][:, 0:w], beta[k % R][:, 0:w], left[k % R][:, 1:w + 1],
                                                ALU.mult).then_inc(weighed, 1)

            @block.vector
            def _(dve):
                dve.sem_inc(turned, R)
                dve.sem_inc(weighed, R)
                for j in range(2):
                    dve.sem_inc(y_stored[j], 16)

                with dve.Fori(0, steps) as i:
                    def scan(k):
                        g = gs[k]
                        w = g.m * P
                        dst = left[k % R]
                        dve.wait_ge(weighed, i * NG + k + 1)
                        if g.first:
                            ins = nc.vector.memset(dst[:, w:w + 1], 1.0)
                        else:
                            dve.wait_ge(scanned, i * NG + k)
                            ins = nc.vector.tensor_copy(dst[:, w:w + 1], left[(k - 1) % R][:, 0:1])
                        ins.then_inc(edge, 1)
                        dve.wait_ge(edge, i * NG + k + 1)
                        dve.wait_ge(squashed, i * NG + k + 5)
                        kr = keep[k % R][:, 0:w][:, ::-1]
                        nc.vector.tensor_tensor_scan(out=dst[:, 0:w][:, ::-1], data0=kr, data1=kr,
                                                     initial=dst[:, w:w + 1], op0=ALU.mult, op1=ALU.min
                                                     ).then_inc(scanned, 1)

                    def output(ui):
                        u = units[ui]
                        if ui % (NU // 2) == 0:
                            dve.wait_ge(y_stored[u.j], i * 16 + 16)
                            dve.wait_ge(loaded[u.j], i * 64 + 64)
                        dve.wait_ge(fed, i * NG + u.first + u.ng - 1 + 5)
                        cc = slice(HD * u.hh, HD * u.hh + HD)
                        nc.vector.tensor_tensor(y[u.j][:, u.b, cc], o_ps[ui % 2][:, 0:HD], gt[u.j][:, u.b, cc],
                                                ALU.mult).then_inc(out_made, 1)
                        if ui % (NU // 2) == NU // 2 - 1:
                            dve.wait_ge(out_made, i * NU + ui + 3)
                            dve.sem_inc(pair_done, 1)

                    for k in range(LEAD - 1):
                        scan(k)
                    for n in range(NG + 2):
                        if n + LEAD - 1 < NG:
                            scan(n + LEAD - 1)
                        if n < NG and who[n] == "v":
                            copy_out(dve, nc.vector.tensor_copy, i, n)
                        if n >= 2 and gs[n - 2].last:
                            output(gs[n - 2].ui)


def index_scores(nc, c, fm, wi, scores):
    units = [(j, hh, b, a, m) for j in range(2) for hh in range(2) for b in range(2, NT)
             for a, m in chunks(b + 1, PB)]
    NU = len(units)
    per_head = NU // 4
    steps = I_HEADS // 4
    assert NU % 4 == 0
    with Scope(nc) as sc:
        q = [sc.sb(f"q{k}", [P, S]) for k in range(2)]
        kk = sc.sb("k", [P, S])
        w_raw = sc.sb("w_raw", [P, NT, I_HEADS])
        w = sc.sb("w", [P, NT, I_HEADS])
        pos = [sc.sb(f"pos{k}", [P, PIECE]) for k in range(4)]
        s_ps = [sc.ps(f"s{k}", [P, PIECE]) for k in range(4)]
        loaded = sc.sems("loaded", 2)
        keys_in = sc.sem("keys_in")
        w_in = sc.sem("w_in")
        w_made = sc.sem("w_made")
        scored = sc.sem("scored")
        clipped = sc.sem("clipped")
        added = sc.sem("added")
        with nc.Block() as block:
            @block.sync
            def _(sp):
                sp.dma_start(w_raw[:], wi.rearrange("(t p) n -> p t n", p=P)).then_inc(w_in, 16)
                for r in range(2):
                    sp.dma_start(kk[r * HD:(r + 1) * HD, :], fm[FM1["ki"] * P:FM1["ki"] * P + HD, :]
                                 ).then_inc(keys_in, 16)
                sp.sem_inc(scored, NU)
                with sp.Fori(0, steps) as i:
                    for j in range(2):
                        sp.wait_ge(scored, i * NU + (j + 1) * (NU // 2))
                        sp.dma_start(q[j][:], fm[bass.ds((i * 2 + j + FM1["qi"]) * P, P), :]).then_inc(loaded[j], 16)

            @block.tensor
            def _(pe):
                pe.sem_inc(clipped, 4)
                pe.wait_ge(keys_in, 32)
                with pe.Fori(0, steps) as i:
                    for ui, (j, hh, b, a, m) in enumerate(units):
                        r = slice(HD * hh, HD * hh + HD)
                        if ui % (NU // 2) == 0:
                            pe.wait_ge(loaded[j], i * 16 + 16)
                        pe.wait_ge(clipped, i * NU + ui + 1)
                        for x, wd in chunks(m * P, BANK):
                            last = nc.tensor.matmul(s_ps[ui % 4][:, x:x + wd], q[j][r, b * P:(b + 1) * P],
                                                    kk[r, a * P + x:a * P + x + wd], start=True, stop=True)
                        last.then_inc(scored, 1)

            @block.scalar
            def _(act):
                with act.Fori(0, steps) as i:
                    for ui, (j, hh, b, a, m) in enumerate(units):
                        act.wait_ge(scored, i * NU + ui + 1 + NU)
                        act.wait_ge(added, i * NU + ui + 1 + per_head)
                        nc.scalar.activation(pos[ui % 4][:, 0:m * P], s_ps[ui % 4][:, 0:m * P], ACT.Relu
                                             ).then_inc(clipped, 1)

            @block.vector
            def _(dve):
                for b in range(2, NT):
                    nc.vector.memset(scores(b), 0.0)
                dve.wait_ge(w_in, 16)
                nc.vector.tensor_scalar(w[:], w_raw[:], IDX_SCALE, None, ALU.mult).then_inc(w_made, 1)
                dve.wait_ge(w_made, 1)
                dve.sem_inc(added, 4 + per_head)
                with dve.Fori(0, steps) as i:
                    for ui, (j, hh, b, a, m) in enumerate(units):
                        dst = scores(b)[:, a * P:(a + m) * P]
                        dve.wait_ge(clipped, i * NU + ui + 5)
                        dve.wait_ge(added, i * NU + ui + 5)
                        nc.vector.scalar_tensor_tensor(
                            out=dst, in0=pos[ui % 4][:, 0:m * P],
                            scalar=w[:, b, bass.ds(i * 4 + j * 2 + hh, 1)], in1=dst, op0=ALU.mult, op1=ALU.add
                        ).then_inc(added, 1)


def select_keys(nc, c, scores, all_scores):
    B0 = TOPK // P
    NB = NT - B0
    with Scope(nc) as sc:
        junk = [sc.sb(f"junk{k}", [P, S], BF16) for k in range(2)]
        even = sc.sb("even", [P, S])
        rank = sc.sb("rank", [P, S])
        best = sc.sb("best", [P, NB], U32)
        bit = sc.sb("bit", [P, NB], U32)
        cand = sc.sb("cand", [P, NB], U32)
        flip = sc.sb("flip", [P, NB], U32)
        thr = sc.sb("thr", [P, NB], U32)
        cnt = sc.sb("cnt", [P, NB])
        enough = sc.sb("enough", [P, NB], U32)
        room = sc.sb("room", [P, NB])
        ch = sc.sem("ch")
        counted = sc.sem("counted")
        pre = sc.sem("pre")
        post = sc.sem("post")
        PER = 6
        with nc.Block() as block:
            @block.vector
            def _(dve):
                v = nc.vector
                for b in range(NT):
                    L = (b + 1) * P
                    if b < B0:
                        v.tensor_copy(scores(b), c.neg_dist[:, S - L:S]).then_inc(pre, 1)
                        dve.wait_ge(pre, b + 1)
                    v.memset(scores(b)[0:HD, L - HD:L], MASKED if b < B0 else NEVER).then_inc(post, 1)
                dve.wait_ge(post, NT)
                v.memset(best[:], 0)
                v.memset(bit[:], SIGN).then_inc(pre, 1)
                dve.wait_ge(pre, B0 + 1)

                def as_float(i, n, src):
                    v.tensor_scalar(flip[:], src[:], 31, 0xFFFFFFFF, ALU.arith_shift_right, ALU.bitwise_xor
                                    ).then_inc(ch, 1)
                    dve.wait_ge(ch, i * PER + n + 1)
                    v.tensor_scalar(flip[:], flip[:], SIGN, None, ALU.bitwise_or).then_inc(ch, 1)
                    dve.wait_ge(ch, i * PER + n + 2)
                    v.tensor_tensor(thr[:], src[:], flip[:], ALU.bitwise_xor).then_inc(ch, 1)
                    dve.wait_ge(ch, i * PER + n + 3)

                with dve.Fori(0, 32) as i:
                    v.tensor_tensor(cand[:], best[:], bit[:], ALU.bitwise_or).then_inc(ch, 1)
                    dve.wait_ge(ch, i * PER + 1)
                    as_float(i, 1, cand)
                    for n in range(NB):
                        b = n + B0
                        if n >= 2:
                            dve.wait_ge(counted, i * NB + n - 1)
                        v.tensor_scalar(junk[n % 2][:, 0:(b + 1) * P], scores(b), thr[:, n:n + 1].bitcast(F32),
                                        None, ALU.is_ge, ALU.add, accum_out=cnt[:, n:n + 1]).then_inc(counted, 1)
                    dve.wait_ge(counted, i * NB + NB)
                    v.tensor_scalar(enough[:], cnt[:], TOPK - 0.5, None, ALU.is_ge).then_inc(ch, 1)
                    dve.wait_ge(ch, i * PER + 5)
                    v.tensor_scalar(bit[:], bit[:], 1, None, ALU.logical_shift_right)
                    v.copy_predicated(best[:], enough[:], cand[:]).then_inc(ch, 1)
                    dve.wait_ge(ch, i * PER + 6)
                as_float(32, 0, best)
                base = 32 * PER + 3
                for n in range(NB):
                    b = n + B0
                    L = (b + 1) * P
                    t = thr[:, n:n + 1].bitcast(F32)
                    sc_b = scores(b)
                    v.tensor_scalar(junk[0][:, 0:L], sc_b, t, None, ALU.is_gt, ALU.add, accum_out=cnt[:, n:n + 1])
                    v.tensor_scalar(even[:, 0:L], sc_b, t, None, ALU.is_equal).then_inc(ch, 1)
                    base += 1
                    dve.wait_ge(ch, base)
                    v.tensor_scalar(room[:, n:n + 1], cnt[:, n:n + 1], -1.0, float(TOPK), ALU.mult, ALU.add)
                    v.tensor_tensor_scan(out=rank[:, 0:L], data0=even[:, 0:L], data1=even[:, 0:L], initial=0.0,
                                         op0=ALU.add, op1=ALU.max).then_inc(ch, 1)
                    base += 1
                    dve.wait_ge(ch, base)
                    v.scalar_tensor_tensor(out=even[:, 0:L], in0=rank[:, 0:L], scalar=room[:, n:n + 1],
                                           in1=even[:, 0:L], op0=ALU.is_le, op1=ALU.mult).then_inc(ch, 1)
                    base += 1
                    dve.wait_ge(ch, base)
                    v.scalar_tensor_tensor(out=rank[:, 0:L], in0=sc_b, scalar=t, in1=even[:, 0:L],
                                           op0=ALU.is_gt, op1=ALU.add).then_inc(ch, 1)
                    base += 1
                    dve.wait_ge(ch, base)
                    v.tensor_scalar(even[:, 0:L], rank[:, 0:L], -1.0, -MASKED, ALU.add, ALU.mult).then_inc(ch, 1)
                    base += 1
                    dve.wait_ge(ch, base)
                    v.tensor_tensor(sc_b, even[:, 0:L], c.neg_dist[:, S - L:S], ALU.add).then_inc(ch, 1)
                    base += 1
                    dve.wait_ge(ch, base)


def out_project(nc, c, y_dram, w_out, resid, dst):
    KY = YW // P
    half = NT // 2
    with Scope(nc) as sc:
        w = sc.sb("w", [P, KY, D])
        y = [sc.sb(f"y{k}", [P, YW]) for k in range(2)]
        x = [sc.sb(f"x{k}", [P, D]) for k in range(2)]
        h = [sc.sb(f"h{k}", [P, D]) for k in range(2)]
        yT = [sc.sb(f"yT{k}", [P, YW]) for k in range(2)]
        t_ps = sc.ps("t", [P, 3 * BANK])
        o_ps = [sc.ps(f"o{k}", [P, D]) for k in range(2)]
        w_in = sc.sem("w_in")
        y_in = sc.sems("y_in", 2)
        x_in = sc.sems("x_in", 2)
        turned = sc.sem("turned")
        taken = sc.sem("taken")
        summed = sc.sem("summed")
        added = sc.sem("added")
        stored = sc.sems("stored", 2)
        with nc.Block() as block:
            @block.sync
            def _(sp):
                sp.dma_start(w[:], w_out.rearrange("(k p) n -> p k n", p=P)).then_inc(w_in, 16)

                def load(n, k, d, to, arrived):
                    sp.dma_start(to[k][:], d[bass.ds(n * P, P), :]).then_inc(arrived[k], 16)

                def store(n, k):
                    sp.dma_start(dst[bass.ds(n * P, P), :], h[k][:]).then_inc(stored[k], 16)

                for k in range(2):
                    load(k, k, y_dram, y, y_in)
                    load(k, k, resid, x, x_in)
                with sp.Fori(0, half - 1) as i:
                    for k in range(2):
                        n = i * 2 + k + 2
                        sp.wait_ge(turned, n + 1)
                        load(n, k, y_dram, y, y_in)
                        sp.wait_ge(added, n + 1)
                        load(n, k, resid, x, x_in)
                        store(n - 2, k)
                for k in range(2):
                    sp.wait_ge(added, NT + k + 1)
                    store(NT - 2 + k, k)
                    sp.wait_ge(stored[k], 16 * (half + 1))

            @block.tensor
            def _(pe):
                pe.sem_inc(turned, 2)
                pe.sem_inc(taken, 1)

                def turn(i, k):
                    pe.wait_ge(y_in[k], i * 16 + 16)
                    pe.wait_ge(taken, i * 2 + k + 1)
                    for j in range(KY):
                        last = nc.tensor.transpose(t_ps[:, j * P:(j + 1) * P], y[k][:, j * P:(j + 1) * P], c.ident[:])
                    last.then_inc(turned, 1)

                def product(i, k):
                    pe.wait_ge(taken, i * 2 + k + 2)
                    pe.wait_ge(added, i * 2 + k + 1)
                    for x0 in range(0, D, BANK):
                        for j in range(KY):
                            last = nc.tensor.matmul(o_ps[k][:, x0:x0 + BANK], yT[k][:, j * P:(j + 1) * P],
                                                    w[:, j, x0:x0 + BANK], start=(j == 0), stop=(j == KY - 1))
                    last.then_inc(summed, 1)

                turn(0, 0)
                pe.wait_ge(w_in, 16)
                with pe.Fori(0, half - 1) as i:
                    turn(i, 1)
                    product(i, 0)
                    turn(i + 1, 0)
                    product(i, 1)
                turn(half - 1, 1)
                product(half - 1, 0)
                product(half - 1, 1)

            @block.scalar
            def _(act):
                act.sem_inc(summed, 2)
                with act.Fori(0, half) as i:
                    for k in range(2):
                        n = i * 2 + k
                        act.wait_ge(summed, n + 1)
                        act.wait_ge(turned, n + 3)
                        nc.scalar.copy(yT[k][:], t_ps[:, 0:YW]).then_inc(taken, 1)

            @block.vector
            def _(dve):
                dve.sem_inc(added, 2)
                for k in range(2):
                    dve.sem_inc(stored[k], 16)
                with dve.Fori(0, half) as i:
                    for k in range(2):
                        n = i * 2 + k
                        dve.wait_ge(summed, n + 3)
                        dve.wait_ge(x_in[k], i * 16 + 16)
                        dve.wait_ge(stored[k], i * 16 + 16)
                        nc.vector.tensor_tensor(h[k][:], o_ps[k][:], x[k][:], ALU.add).then_inc(added, 1)


def memory_kv(nc, c, mem, gain, w_fm, w_v, km, vm):
    with Scope(nc) as sc:
        memT = sc.sb("memT", [P, D // P, MEM])
        norm_rows(nc, c, mem, gain, MEM, D, dstT=memT)
        project(nc, memT, D // P, MEM, w_fm, 2, c.fm_one, km, [(w_v, vm, 2 * P, False)])


def token_view(d, col, w):
    return d.rearrange("(t p) n -> p t n", p=P)[:, :, bass.ds(col, w)]


def memory_attention(nc, c, fm, km, vm, gm, y, ycol):
    def loads(i, j):
        pair = i * 2 + j
        return (fm[bass.ds((pair + FM0["qm"]) * P, P), :], [km[bass.ds(pair * P, P), :]],
                token_view(vm, pair * P, P), token_view(gm, pair * P, P))

    softmax_attention(nc, c, 1, [(b, [0, 1]) for b in range(NT)], loads, MEM,
                      lambda i, j: token_view(y, (i * 2 + j) * P + ycol, P), c.scale_m, None,
                      lambda u: c.zero_bias[:])


def trunk(nc, a, out):
    def dram(name, shape):
        return nc.dram_tensor(name, shape, F32, kind="Internal").ap()

    x, mem = a["x"][0], a["mem"][0]
    fm0, fm1 = dram("fm0", (NFM * P, S)), dram("fm1", (NFM * P, S))
    va, ga = dram("va", (S, P)), dram("ga", (S, A_HEADS * HD))
    vb, gb = dram("vb", (S, B_HEADS * HD)), dram("gb", (S, B_HEADS * HD))
    gm0, gm1 = dram("gm0", (S, M_HEADS * HD)), dram("gm1", (S, M_HEADS * HD))
    km0, km1, vm0, vm1 = (dram(n, (MEM, MEM)) for n in ("km0", "km1", "vm0", "vm1"))
    y0, y1 = dram("y0", (S, YW)), dram("y1", (S, YW))
    h1, h2 = dram("h1", (S, D)), dram("h2", (S, D))
    ckv, wi, gc = dram("ckv", (S, LAT)), dram("wi", (S, I_HEADS)), dram("gc", (S, C_HEADS * HD))
    kc, vc = dram("kc", (C_HEADS * HD, S)), dram("vc", (S, C_HEADS * HD))

    with Scope(nc) as top:
        c = make_constants(nc, top, a["e_sinks"])

        memory_kv(nc, c, mem, a["e_mem_norm"], a["e_mem_k"], a["e_w_mem_kv"][0][:, MEM:2 * MEM], km0, vm0)
        memory_kv(nc, c, mem, a["o_mem_norm"], a["o_mem_k"], a["o_w_mem_kv"][0][:, MEM:2 * MEM], km1, vm1)
        with Scope(nc) as sc:
            hT = sc.sb("hT", [P, D // P, S])
            norm_rows(nc, c, x, a["e_norm"], S, D, dstT=hT)
            w = a["e_w_in"][0]
            project(nc, hT, D // P, S, a["e_fm"], NFM, c.fm_scale0, fm0,
                    [(w[:, 640:768], va, 128, False), (w[:, 768:1280], ga, 512, True),
                     (w[:, 2304:2816], vb, 512, False), (w[:, 2816:3328], gb, 512, True),
                     (w[:, 3584:3840], gm0, 256, True)])

        def loads_a(i, j):
            return (fm0[bass.ds((i * 2 + j + FM0["qa"]) * P, P), :],
                    [fm0[bass.ds(i * HD + FM0["ka"] * P, HD), :] for _ in range(2)],
                    token_view(va, i * HD, HD), token_view(ga, (i * 2 + j) * P, P))

        softmax_attention(nc, c, 2, [(b, list(range(max(b - 1, 0), b + 1))) for b in range(NT)], loads_a, S,
                          lambda i, j: token_view(y0, (i * 2 + j) * P, P), c.slope_a, c.sink,
                          lambda u: c.window[:, 0 if u.b else P:2 * P], v_shared=True)
        stick_breaking(nc, c, fm0, vb, gb, y0)
        memory_attention(nc, c, fm0, km0, vm0, gm0, y0, (A_HEADS + B_HEADS) * HD)
        out_project(nc, c, y0, a["e_w_out"][0], x, h1)

        with Scope(nc) as sc:
            hT = sc.sb("hT", [P, D // P, S])
            norm_rows(nc, c, h1, a["o_norm"], S, D, dstT=hT)
            w = a["o_w_in"][0]
            project(nc, hT, D // P, S, a["o_fm"], NFM, c.fm_scale1, fm1,
                    [(w[:, 1024:1280], ckv, 256, False), (w[:, 1856:1864], wi, 8, False),
                     (w[:, 1864:2376], gc[:, 0:512], 512, True), (w[:, 2376:2888], gc[:, 512:1024], 512, True),
                     (w[:, 3144:3400], gm1, 256, True)])
        with Scope(nc) as sc:
            cT = sc.sb("cT", [P, LAT // P, S])
            norm_rows(nc, c, ckv, a["o_kv_norm"], S, LAT, dstT=cT)
            uv = a["o_w_uv"][0].rearrange("l h d -> l (h d)")
            project(nc, cT, LAT // P, S, a["o_uk"], 8, c.fm_one, kc,
                    [(uv[:, 0:512], vc[:, 0:512], 512, False), (uv[:, 512:1024], vc[:, 512:1024], 512, False)])
        memory_attention(nc, c, fm1, km1, vm1, gm1, y1, C_HEADS * HD)
        with Scope(nc) as sc:
            all_scores = sc.sb("scores", [P, P * (NT * (NT + 1) // 2)])

            def scores(b):
                o = P * (b * (b + 1) // 2)
                return all_scores[:, o:o + (b + 1) * P]

            index_scores(nc, c, fm1, wi, scores)
            select_keys(nc, c, scores, all_scores)

            def loads_c(i, j):
                pair = i * 2 + j
                return (fm1[bass.ds((pair + FM1["qc"]) * P, P), :], [kc[bass.ds(pair * P, P), :]],
                        token_view(vc, pair * P, P), token_view(gc, pair * P, P))

            softmax_attention(nc, c, C_HEADS // 4, [(b, list(range(b + 1))) for b in range(NT)], loads_c, S,
                              lambda i, j: token_view(y1, (i * 2 + j) * P, P), c.slope_c, None,
                              lambda u: scores(u.b))
        out_project(nc, c, y1, a["o_w_out"][0], h1, h2)
        norm_rows(nc, c, h2, a["final_norm"].rearrange("(a n) -> a n", a=1), S, D, out=out[0])


def tiles(w, starts):
    import numpy as np
    return np.ascontiguousarray(np.stack([w[:, s:s + P].reshape(-1, P, P).transpose(1, 0, 2) for s in starts]))


def kernel(**inputs):
    import numpy as _np
    import concourse.bacc as _bacc
    from concourse import mybir as _mybir
    from concourse.bass_utils import run_bass_kernel_spmd as _run

    nc = _bacc.Bacc("TRN2", target_bir_lowering=False, num_devices=1)
    arrays = {k: _np.ascontiguousarray(v) for k, v in inputs.items()}
    e, o = arrays["e_w_in"][0], arrays["o_w_in"][0]
    arrays["e_fm"] = tiles(e, [0, 128, 256, 384, 512] + list(range(1280, 2304, 128)) + [3328, 3456])
    arrays["o_fm"] = tiles(o, list(range(0, 1024, 128)) + list(range(1280, 1793, 128)) + [2888, 3016])
    arrays["e_mem_k"] = tiles(arrays["e_w_mem_kv"][0], [0, 128])
    arrays["o_mem_k"] = tiles(arrays["o_w_mem_kv"][0], [0, 128])
    arrays["o_uk"] = tiles(arrays.pop("o_w_uk")[0].reshape(LAT, C_HEADS * HD), list(range(0, 1024, 128)))
    aps = {k: nc.dram_tensor("in_" + k, v.shape, _mybir.dt.from_np(v.dtype), kind="ExternalInput").ap()
           for k, v in arrays.items()}
    out = nc.dram_tensor("out_0", (1, S, D), _mybir.dt.float32, kind="ExternalOutput").ap()
    trunk(nc, aps, out)
    r = _run(nc, [{"in_" + k: v for k, v in arrays.items()}], core_ids=[0])
    return r.results[0]["out_0"]
```

```python
from contextlib import ExitStack

import concourse.bass as bass
from concourse import mybir

F32 = mybir.dt.float32
BF16 = mybir.dt.bfloat16
F32R = mybir.dt.float32r
I32 = mybir.dt.int32
U32 = mybir.dt.uint32
U8 = mybir.dt.uint8
ALU = mybir.AluOpType
ACT = mybir.ActivationFunctionType
AX_X = mybir.AxisListType.X

P = 128
S = 2048
D = 1024
NT = S // P
HD = 64
EPS = 1e-6
MEM = 256
TOPK = 256
LAT = 256
A_HEADS, B_HEADS, C_HEADS, I_HEADS, M_HEADS = 8, 8, 16, 8, 4
SCALE = HD ** -0.5
IDX_SCALE = (HD ** -0.5) * (I_HEADS ** -0.5)
MASKED = -1.0e30
NEVER = -3.0e38
YW = 1280
BANK = 512
SIGN = 0x80000000
PIECE = 1024
PB = PIECE // P
GB = BANK // P

FM0 = {"qa": 0, "ka": 4, "qb": 5, "kb": 9, "qm": 13}
FM1 = {"qi": 0, "ki": 4, "qc": 5, "qm": 13}
NFM = 15
HT = S // 2
BITS1, BITS2 = 12, 26


def slopes(n):
    return [2.0 ** (-8.0 * h / n) for h in range(1, n + 1)]


def chunks(n, w):
    return [(a, min(w, n - a)) for a in range(0, n, w)]


class Scope:

    made = 0

    def __init__(self, nc):
        self.nc = nc
        self.ctx = ExitStack()
        Scope.made += 1
        self.tag = f"s{Scope.made}_"
        self.taken = []

    def __enter__(self):
        return self

    def __exit__(self, *e):
        if self.taken and e[0] is None:
            with self.nc.Block() as block:
                @block.sync
                def _(sp):
                    for s in self.taken:
                        sp.sem_clear(s)
        self.ctx.close()

    def close(self):
        self.__exit__(None, None, None)

    def sb(self, name, shape, dt=F32, side=None):
        return self.ctx.enter_context(self.nc.sbuf_tensor(self.tag + name, shape, dt, side=side))

    def ps(self, name, shape, dt=F32):
        return self.ctx.enter_context(self.nc.psum_tensor(self.tag + name, shape, dt))

    def sem(self, name):
        self.taken.append(self.ctx.enter_context(self.nc.semaphore(self.tag + name)))
        return self.taken[-1]

    def sems(self, name, n):
        return [self.sem(f"{name}{k}") for k in range(n)]


class Constants:
    pass


def distances(nc, out, W):
    with Scope(nc) as sc:
        ramp = sc.sb("ramp", [P, W], I32)
        ramp_made = sc.sem("ramp_made")
        floats_made = sc.sem("floats_made")
        with nc.Block() as block:
            @block.gpsimd
            def _(pool):
                nc.gpsimd.iota(ramp[:], pattern=[[-1, W]], base=W - P, channel_multiplier=1).then_inc(ramp_made, 1)

            @block.vector
            def _(dve):
                dve.wait_ge(ramp_made, 1)
                nc.vector.tensor_copy(out[:], ramp[:]).then_inc(floats_made, 1)
                dve.wait_ge(floats_made, 1)
                nc.vector.scalar_tensor_tensor(out=out[:], in0=out[:], scalar=-1.0, in1=out[:],
                                               op0=ALU.mult, op1=ALU.min)


def make_constants(nc, sc, e_sinks):
    c = Constants()
    c.ident = sc.sb("ident", [P, P])
    c.identb = sc.sb("identb", [P, P], BF16)
    c.causal = sc.sb("causal", [P, P], BF16)
    c.window = sc.sb("window", [P, 2 * P])
    c.zero_bias = sc.sb("zero_bias", [P, MEM])
    c.slope_a = sc.sb("slope_a", [P, A_HEADS])
    c.slope_c = sc.sb("slope_c", [P, C_HEADS])
    c.scale_m = sc.sb("scale_m", [P, M_HEADS])
    c.fm_scale0 = sc.sb("fm_scale0", [P, 16])
    c.fm_scale1 = sc.sb("fm_scale1", [P, 16])
    c.fm_one = sc.sb("fm_one", [P, 8])
    c.sink = sc.sb("sink", [P, A_HEADS])
    distances(nc, c.window, 2 * P)
    with Scope(nc) as st:
        cleared = st.sem("cleared")
        sinks_in = st.sem("sinks_in")
        with nc.Block() as block:
            @block.gpsimd
            def _(pool):
                for t in (c.ident, c.identb, c.causal):
                    nc.gpsimd.memset(t[:], 0.0).then_inc(cleared, 1)
                pool.wait_ge(cleared, 3)
                for t in (c.ident, c.identb):
                    nc.gpsimd.affine_select(out=t[:], in_=t[:], compare_op=ALU.not_equal, fill=1.0, base=0,
                                            pattern=[[-1, P]], channel_multiplier=1)
                nc.gpsimd.affine_select(out=c.causal[:], in_=c.causal[:], compare_op=ALU.is_gt, fill=MASKED,
                                        base=0, pattern=[[-1, P]], channel_multiplier=1)

            @block.sync
            def _(sp):
                sp.dma_start(c.sink[:], e_sinks[0:1, :].broadcast_to([P, A_HEADS])).then_inc(sinks_in, 16)
                sp.wait_ge(sinks_in, 16)

            @block.vector
            def _(dve):
                v = nc.vector
                v.memset(c.window[0:64, 0:64], MASKED)
                v.memset(c.window[64:128, 0:128], MASKED)
                v.memset(c.window[0:64, 192:256], MASKED)
                v.memset(c.zero_bias[:], 0.0)
                for t, n in ((c.slope_a, A_HEADS), (c.slope_c, C_HEADS)):
                    for h, s in enumerate(slopes(n)):
                        v.memset(t[:, h:h + 1], s)
                v.memset(c.scale_m[:], SCALE)
                v.memset(c.fm_scale0[:, 4:16], 1.0)
                v.memset(c.fm_scale1[:, 0:FM1["qc"]], 1.0)
                v.memset(c.fm_scale1[:, FM1["qm"]:16], 1.0)
                v.memset(c.fm_one[:], 1.0)
                for t, n, first in ((c.fm_scale0, A_HEADS, FM0["qa"]), (c.fm_scale1, C_HEADS, FM1["qc"])):
                    for h, s in enumerate(slopes(n)):
                        col = first + h // 2
                        v.memset(t[HD * (h % 2):HD * (h % 2) + HD, col:col + 1], SCALE / s)
    return c


def norm_rows(nc, c, src, gain, T, W, dstT=None, out=None):
    nt, kt = T // P, W // P
    half = nt // 2
    with Scope(nc) as sc:
        x = sc.sb("x", [P, nt, W])
        g = sc.sb("g", [P, W])
        xn = sc.sb("xn", [P, 2, W])
        ss = sc.sb("ss", [P, nt])
        rms = sc.sb("rms", [P, nt])
        rstd = sc.sb("rstd", [P, nt])
        tp = [sc.ps(f"tp{k}", [P, max(W, BANK)]) for k in range(2)]
        x_in = sc.sems("x_in", 2)
        g_in = sc.sem("g_in")
        squared = sc.sem("squared")
        mean_made = sc.sem("mean_made")
        root_made = sc.sem("root_made")
        rstd_made = sc.sem("rstd_made")
        normed = sc.sem("normed")
        turned = sc.sem("turned")
        hi_made = sc.sem("hi_made")
        evacuated = sc.sem("evacuated")
        stored = sc.sems("stored", 2)
        xv = src.rearrange("(t p) d -> p t d", p=P)
        with nc.Block() as block:
            @block.sync
            def _(sp):
                for k in range(2):
                    sp.dma_start(x[:, k * half:(k + 1) * half, :], xv[:, k * half:(k + 1) * half, :]
                                 ).then_inc(x_in[k], 16)
                sp.dma_start(g[:], gain.broadcast_to([P, W])).then_inc(g_in, 16)
                if out is not None:
                    with sp.Fori(0, half) as i:
                        for k in range(2):
                            sp.wait_ge(normed, i * 2 + k + 1)
                            sp.dma_start(out[bass.ds((i * 2 + k) * P, P), :], xn[:, k, :]).then_inc(stored[k], 16)
                    for k in range(2):
                        sp.wait_ge(stored[k], 16 * (half + 1))

            @block.scalar
            def _(act):
                for t in range(nt):
                    if t % half == 0:
                        act.wait_ge(x_in[t // half], 16)
                    if t >= 2:
                        act.wait_ge(squared, t - 1)
                    nc.scalar.activation(xn[:, t % 2, :], x[:, t, :], ACT.Square, accum_out=ss[:, t:t + 1]
                                         ).then_inc(squared, 1)
                act.wait_ge(mean_made, 1)
                nc.scalar.activation(rms[:], rms[:], ACT.Sqrt).then_inc(root_made, 1)
                if dstT is not None:
                    with act.Fori(0, half) as i:
                        for k in range(2):
                            act.wait_ge(turned, i * 2 + k + 1 + 2)
                            nc.scalar.copy(dstT[0][:, :, bass.ds((i * 2 + k) * P, P)],
                                           tp[k][:, 0:W].rearrange("p (k t) -> p k t", k=kt)
                                           ).then_inc(hi_made, 1)

            @block.vector
            def _(dve):
                dve.wait_ge(squared, nt)
                nc.vector.tensor_scalar(rms[:], ss[:], 1.0 / W, EPS, ALU.mult, ALU.add).then_inc(mean_made, 1)
                dve.wait_ge(root_made, 1)
                nc.vector.reciprocal(rstd[:], rms[:]).then_inc(rstd_made, 1)
                dve.wait_ge(rstd_made, 1)
                dve.wait_ge(g_in, 16)
                for k in range(2):
                    dve.wait_ge(x_in[k], 16)
                if dstT is not None:
                    dve.sem_inc(turned, 2)
                else:
                    for k in range(2):
                        dve.sem_inc(stored[k], 16)

                def normalize(i, k):
                    if dstT is not None:
                        dve.wait_ge(turned, i * 2 + k + 1)
                    else:
                        dve.wait_ge(stored[k], i * 16 + 16)
                    nc.vector.scalar_tensor_tensor(
                        out=xn[:, k, :], in0=x[:, bass.ds(i * 2 + k, 1), :].rearrange("p a d -> p (a d)"),
                        scalar=rstd[:, bass.ds(i * 2 + k, 1)], in1=g[:], op0=ALU.mult, op1=ALU.mult
                    ).then_inc(normed, 1)

                def low_part(i, k):
                    dve.wait_ge(hi_made, i * 2 + k + 1)
                    at = bass.ds((i * 2 + k) * P, P)
                    nc.vector.tensor_tensor(dstT[1][:, :, at], tp[k][:, 0:W].rearrange("p (k t) -> p k t", k=kt),
                                            dstT[0][:, :, at].bitcast(F32), ALU.subtract).then_inc(evacuated, 1)

                if dstT is None:
                    with dve.Fori(0, half) as i:
                        for k in range(2):
                            normalize(i, k)
                else:
                    normalize(0, 0)
                    if half > 1:
                        with dve.Fori(0, half - 1) as i:
                            normalize(i, 1)
                            low_part(i, 0)
                            normalize(i + 1, 0)
                            low_part(i, 1)
                    normalize(half - 1, 1)
                    low_part(half - 1, 0)
                    low_part(half - 1, 1)

            if dstT is not None:
                @block.tensor
                def _(pe):
                    pe.sem_inc(evacuated, 2)
                    with pe.Fori(0, half) as i:
                        for k in range(2):
                            pe.wait_ge(normed, i * 2 + k + 1)
                            pe.wait_ge(evacuated, i * 2 + k + 1)
                            for j in range(kt):
                                last = nc.tensor.transpose(tp[k][:, j * P:(j + 1) * P], xn[:, k, j * P:(j + 1) * P],
                                                           c.ident[:])
                            last.then_inc(turned, 1)


def in_pairs(eng, n, body):
    if n // 2 > 1:
        with eng.Fori(0, n // 2) as i:
            for k in range(2):
                body(i, k)
    elif n // 2 == 1:
        for k in range(2):
            body(0, k)
    if n % 2:
        body(n // 2, 0)


def split_matmuls(nc, out, sta, mov, last):
    n = len(sta)
    for j, ((sh, sl), (mh, ml)) in enumerate(zip(sta, mov)):
        nc.tensor.matmul(out, sh, mh, start=(j == 0), stop=False)
        nc.tensor.matmul(out, sh, ml, start=False, stop=False)
        ins = nc.tensor.matmul(out, sl, mh, start=False, stop=(j == n - 1))
    ins.then_inc(last, 1)


def project(nc, srcT, KT, T, w_fm, nfm, fm_scale, fm_out, tm_jobs, beside=None, keep=(), fetch=()):
    gw = min(BANK, T)
    ng = T // gw
    nt = T // P
    TG = 2
    WW = 2 * P
    seg = T // len(srcT[0])

    def tokens(j, t0, n):
        return tuple(part[t0 // seg][:, j, t0 % seg:t0 % seg + n] for part in srcT)

    with Scope(nc) as sc:
        w = [sc.sb(f"w{k}", [P, KT, WW]) for k in range(2)]
        wh = [sc.sb(f"wh{k}", [P, KT, WW], F32R) for k in range(2)]
        wl = [sc.sb(f"wl{k}", [P, KT, WW], F32R) for k in range(2)]
        parts = [sc.sb(f"parts{k}", [P, 2, gw], F32R) for k in range(4)]
        scale = sc.sb("scale", [P, 2])
        ready = sc.sb("ready", [P, 1])
        gate = sc.sb("gate", [P, 1])
        rows = [sc.sb(f"rows{k}", [P, TG, WW]) for k in range(2)]
        acc = [sc.ps(f"acc{k}", [P, BANK]) for k in range(4)]
        w_in = sc.sems("w_in", 2)
        set_up = sc.sem("set_up")
        w_hi = sc.sem("w_hi")
        w_split = sc.sem("w_split")
        summed = sc.sem("summed")
        used = sc.sem("used")
        scale_set = sc.sem("scale_set")
        raw_made = sc.sem("raw_made")
        lo_made = sc.sem("lo_made")
        kept = sc.sem("kept")
        fetched = sc.sem("fetched")
        stored = sc.sems("stored", 4)
        rowed = sc.sem("rowed")
        rows_out = sc.sems("rows_out", 2)
        nrow = nt * len(tm_jobs)
        nquad = nrow // TG
        jobs = nfm + len(tm_jobs)
        with nc.Block() as block:
            @block.sync
            def _(sp):
                sp.sem_inc(w_split, 2)
                for t, d in fetch:
                    sp.dma_start(t, d).then_inc(fetched, 16)

                def step(i, k):
                    sp.wait_ge(w_split, i * 2 + k + 1)
                    sp.dma_start(w[k][:, :, 0:P], w_fm[bass.ds(i * 2 + k, 1), :, :, :]
                                 .rearrange("a p k m -> p (a k) m")).then_inc(w_in[k], 16)

                in_pairs(sp, nfm, step)
                for n, (wd, _, width, _) in enumerate(tm_jobs):
                    m = nfm + n
                    sp.wait_ge(w_split, m + 1)
                    sp.dma_start(w[m % 2][:, :, 0:width], wd.rearrange("(k p) n -> p k n", p=P)
                                 ).then_inc(w_in[m % 2], 16)
                for d, t in keep:
                    sp.dma_start(d, t).then_inc(kept, 16)
                if keep:
                    sp.wait_ge(kept, 16 * len(keep))

            def low_parts(i, k):
                for g in range(ng):
                    nc.gpsimd.wait_ge(raw_made, (i * 2 + k) * ng + g + 5)
                    b = (k * ng + g) % 4
                    nc.gpsimd.tensor_tensor(parts[b][:, 1, :], parts[b][:, 1, :].bitcast(F32),
                                            parts[b][:, 0, :].bitcast(F32), ALU.subtract).then_inc(lo_made, 1)

            def weights(eng, ops, low_parts):
                eng.sem_inc(used, 2)
                ops.memset(ready[:], 0.0).then_inc(set_up, 1)
                eng.wait_ge(set_up, 1)

                def split(m, k, round_, width):
                    eng.wait_ge(used, m + 1)
                    eng.wait_ge(w_in[k], round_)
                    ops.tensor_tensor(gate[:], ready[:], ready[:], ALU.add)
                    ops.tensor_copy(wh[k][:, :, 0:width], w[k][:, :, 0:width]).then_inc(w_hi, 1)
                    eng.wait_ge(w_hi, m + 1)
                    ops.tensor_tensor(wl[k][:, :, 0:width], w[k][:, :, 0:width],
                                      wh[k][:, :, 0:width].bitcast(F32), ALU.subtract).then_inc(w_split, 1)

                def split_job(m):
                    if m < jobs:
                        split(m, m % 2, 16 * (m // 2 + 1), tm_jobs[m - nfm][2])

                def step(i, k):
                    low_parts(i, k)
                    split(i * 2 + k + 2, k, i * 16 + 32, P)

                for m in range(2):
                    split(m, m, 16, P)
                in_pairs(eng, nfm - 2, step)
                for n in range(nfm - 2, nfm):
                    low_parts(n // 2, n % 2)
                    split_job(n + 2)
                for m in range(nfm + 2, jobs):
                    split_job(m)

            if beside:
                @block.gpsimd
                def _(pool):
                    weights(pool, nc.gpsimd, low_parts)

                block.vector(beside)
            else:
                @block.gpsimd
                def _(pool):
                    in_pairs(pool, nfm, low_parts)

                @block.vector
                def _(dve):
                    weights(dve, nc.vector, lambda i, k: None)

            @block.tensor
            def _(pe):
                pe.sem_inc(raw_made, 4)
                if fetch:
                    pe.wait_ge(fetched, 16 * len(fetch))
                pe.sem_inc(rowed, 4)

                def step(i, k):
                    pe.wait_ge(w_split, i * 2 + k + 3)
                    for g in range(ng):
                        r = (i * 2 + k) * ng + g
                        bank = (k * ng + g) % 4
                        pe.wait_ge(raw_made, r + 1)
                        split_matmuls(nc, acc[bank][:, 0:gw],
                                      [(wh[k][:, j, 0:P], wl[k][:, j, 0:P]) for j in range(KT)],
                                      [tokens(j, g * gw, gw) for j in range(KT)], summed)
                    pe.wait_ge(summed, (i * 2 + k) * ng + ng)
                    pe.sem_inc(used, 1)

                in_pairs(pe, nfm, step)
                pe.wait_ge(raw_made, ng * nfm + 4)
                for n, (_, _, width, _) in enumerate(tm_jobs):
                    m = nfm + n
                    pe.wait_ge(w_split, m + 3)
                    for t in range(nt):
                        r = n * nt + t
                        pe.wait_ge(rowed, r + 1)
                        split_matmuls(nc, acc[r % 4][:, 0:width], [tokens(j, t * P, P) for j in range(KT)],
                                      [(wh[m % 2][:, j, 0:width], wl[m % 2][:, j, 0:width]) for j in range(KT)],
                                      summed)
                    pe.wait_ge(summed, ng * nfm + (n + 1) * nt)
                    pe.sem_inc(used, 1)

            @block.scalar
            def _(act):
                for k in range(4):
                    act.sem_inc(stored[k], 16)
                for k in range(2):
                    act.sem_inc(rows_out[k], 16)

                def store(i, k, g):
                    b = (k * ng + g) % 4
                    r = (i * 2 + k) * ng + g
                    act.wait_ge(lo_made, r + 1)
                    act.dma_start(fm_out[:, bass.ds((i * 2 + k) * P, P), g * gw:(g + 1) * gw].rearrange(
                        "n p t -> p n t"), parts[b][:].bitcast(F32)).then_inc(stored[b], 16)

                def step(i, k):
                    nc.scalar.copy(scale[:, k:k + 1], fm_scale[:, bass.ds(i * 2 + k, 1)]).then_inc(scale_set, 1)
                    act.wait_ge(scale_set, i * 2 + k + 1)
                    for g in range(ng):
                        b = (k * ng + g) % 4
                        act.wait_ge(stored[b], (i * 32 + k * 16 + 16) if ng == 4 else (i * 16 + 16))
                        act.wait_ge(summed, (i * 2 + k) * ng + g + 1)
                        nc.scalar.mul(parts[b][:, 0, :], acc[b][:, 0:gw], scale[:, k:k + 1])
                        nc.scalar.mul(parts[b][:, 1, :].bitcast(F32), acc[b][:, 0:gw], scale[:, k:k + 1]
                                      ).then_inc(raw_made, 1)
                        if g:
                            store(i, k, g - 1)
                    store(i, k, ng - 1)

                in_pairs(act, nfm, step)
                for n, (_, od, width, silu) in enumerate(tm_jobs):
                    for t in range(nt):
                        r = n * nt + t
                        q = r // TG
                        if r % TG == 0:
                            act.wait_ge(rows_out[q % 2], 16 * (q // 2 + 1))
                        act.wait_ge(summed, ng * nfm + r + 1)
                        nc.scalar.activation(rows[q % 2][:, r % TG, 0:width], acc[r % 4][:, 0:width],
                                             ACT.Silu if silu else ACT.Copy).then_inc(rowed, 1)
                        if r % TG == TG - 1:
                            act.wait_ge(rowed, r + 5)
                            act.dma_start(od[(t - TG + 1) * P:(t + 1) * P, :].rearrange("(t p) n -> p t n", p=P),
                                          rows[q % 2][:, :, 0:width]).then_inc(rows_out[q % 2], 16)
                for k in range(4):
                    uses = len([r for r in range(nfm * ng) if (r // ng % 2 * ng + r % ng) % 4 == k])
                    act.wait_ge(stored[k], 16 * (uses + 1))
                for k in range(2):
                    act.wait_ge(rows_out[k], 16 * ((nquad + 1 - k) // 2 + 1))


class Unit:

    def __init__(self, j, hh, b, kbs):
        self.j, self.hh, self.b, self.kbs = j, hh, b, kbs


class Group:

    def __init__(self, ui, u, a, m, first, last):
        self.ui, self.u, self.a, self.m, self.first, self.last = ui, u, a, m, first, last


def groups_of(units, latest_first=False):
    out = []
    for ui, u in enumerate(units):
        parts = chunks(len(u.kbs), GB)
        u.first, u.ng = len(out), len(parts)
        for n, (a, m) in enumerate(reversed(parts) if latest_first else parts):
            out.append(Group(ui, u, a, m, n == 0, n == len(parts) - 1))
    return out


def shares(n, of_vector):
    who = ["v" if of_vector(k) else "s" for k in range(n)]
    return who, [who[:k + 1].count(who[k]) for k in range(n)], {w: who.count(w) for w in "vs"}


def load_head(sp, qs, kh, kl, q_rows, k_rows, arrived, nk):
    for n in range(2):
        half = slice(n * HD, (n + 1) * HD)
        sp.dma_start(qs[half, :].bitcast(F32), q_rows[n]).then_inc(arrived, 16)
        sp.dma_start(kh[half, :].bitcast(F32), k_rows[0]).then_inc(arrived, 16)
        sp.dma_start(kl[half, :].bitcast(F32), k_rows[1]).then_inc(arrived, 16)


def score_group(nc, out, qs, kh, kl, b, k0, w, stop=True):
    qb = qs[:, b * P:(b + 1) * P]
    nc.tensor.matmul(out, qb, kh[:, k0:k0 + w], start=True, stop=False)
    return nc.tensor.matmul(out, qb, kl[:, k0:k0 + w], start=False, stop=stop)


def transpose_group(nc, c, t_ps, probs, g, turned):
    for x in range(g.m):
        last = nc.tensor.transpose(t_ps[:, x * P:(x + 1) * P], probs[:, x * P:(x + 1) * P], c.ident[:])
    last.then_inc(turned, 1)


def values_group(nc, o_ps, pT, v, g, vc, fed):
    for x in range(g.m):
        for r in range(0, P, HD):
            last = nc.tensor.matmul(o_ps[r:r + HD, 0:HD], pT[:, x * P + r:x * P + r + HD],
                                    v[:, g.u.kbs[g.a + x], vc:vc + HD],
                                    start=(g.first and x == 0), stop=(g.last and x == g.m - 1),
                                    skip_group_check=True)
    last.then_inc(fed, 1)


def softmax_attention(nc, c, steps, per_pair, loads, NK, y_out, scale_tab, sink, bias_of, v_shared=False):
    units = [Unit(j, hh, b, kbs) for j in range(2) for hh in range(2) for b, kbs in per_pair]
    gs = groups_of(units)
    NG, NU, LEAD, EXP_LEAD, R, US = len(gs), len(units), 7, 3, 8, 16
    assert NG % R == 0 and NU % US == 0
    who, nth, per_step = shares(NG, lambda k: k % 16 == 15)
    VW = HD if v_shared else 2 * HD
    with Scope(nc) as sc:
        qs = [sc.sb(f"qs{k}", [P, S], F32R) for k in range(2)]
        kh = [sc.sb(f"kh{k}", [P, NK], F32R) for k in range(2)]
        kl = [sc.sb(f"kl{k}", [P, NK], F32R) for k in range(2)]
        v = [sc.sb(f"v{k}", [P, NK // P, VW]) for k in range(2)]
        gt = [sc.sb(f"g{k}", [P, NT, 2 * HD]) for k in range(2)]
        probs = [sc.sb(f"probs{k}", [P, BANK]) for k in range(R)]
        pT = [sc.sb(f"pT{k}", [P, BANK]) for k in range(4)]
        mx = sc.sb("mx", [P, US, 4])
        top = sc.sb("top", [P, US, 2])
        nmx = sc.sb("nmx", [P, US])
        rsum = sc.sb("rsum", [P, US, 4])
        esink = sc.sb("esink", [P, US])
        den = sc.sb("den", [P, US, 2])
        rden = sc.sb("rden", [P, US])
        gate = sc.sb("gate", [P, US])
        scales = sc.sb("scales", [P, 4])
        sinks = sc.sb("sinks", [P, 4])
        s_ps = [sc.ps(f"s{k}", [P, BANK]) for k in range(4)]
        t_ps = [sc.ps(f"t{k}", [P, BANK]) for k in range(2)]
        o_ps = [sc.ps(f"o{k}", [P, BANK]) for k in range(2)]
        heads_set = sc.sem("heads_set")
        head_in = sc.sems("head_in", 2)
        v_in = sc.sems("v_in", 2)
        g_in = sc.sems("g_in", 2)
        pair_done = sc.sem("pair_done")
        y_stored = sc.sems("y_stored", 2)
        heads_done = sc.sem("heads_done")
        scored = sc.sem("scored")
        biased = sc.sem("biased")
        chain = sc.sem("chain")
        max_made = sc.sem("max_made")
        exp_made = sc.sem("exp_made")
        turned = sc.sem("turned")
        taken = {"s": sc.sem("taken_s"), "v": sc.sem("taken_v")}
        fed = sc.sem("fed")
        out_made = sc.sem("out_made")
        NH = NG // 4
        links = sum((u.ng > 1) + (sink is not None) + (u.ng > 1) + (sink is not None) + 1 for u in units)

        with nc.Block() as block:
            @block.sync
            def _(sp):
                sp.sem_inc(pair_done, 2)
                sp.sem_inc(heads_done, 2)
                for j in range(2):
                    sp.sem_inc(y_stored[j], 16)
                with sp.Fori(0, steps) as i:
                    for j in range(2):
                        for hh in range(2):
                            qd, kd, vd, gd = loads(i, j, hh)
                            sp.wait_ge(heads_done, i * 4 + j * 2 + hh + 1)
                            if hh == 0:
                                sp.wait_ge(y_stored[j], i * 16 + 16)
                            load_head(sp, qs[hh], kh[hh], kl[hh], qd, kd, head_in[hh], NK)
                            if hh == 0:
                                sp.dma_start(v[j][:], vd).then_inc(v_in[j], 16)
                                sp.dma_start(gt[j][:], gd).then_inc(g_in[j], 16)

            @block.tensor
            def _(pe):
                pe.sem_inc(biased, 4)
                pe.sem_inc(taken["s"], 1)
                pe.sem_inc(taken["v"], 1)
                pe.sem_inc(out_made, 2)

                def score(i, k):
                    g = gs[k]
                    u = g.u
                    if k % NH == 0:
                        pe.wait_ge(head_in[u.hh], i * 192 + u.j * 96 + 96)
                    pe.wait_ge(biased, i * NG + k + 1)
                    score_group(nc, s_ps[k % 4][:, 0:g.m * P], qs[u.hh], kh[u.hh], kl[u.hh], u.b,
                                (u.kbs[0] + g.a) * P, g.m * P).then_inc(scored, 1)

                def turn(i, n):
                    pe.wait_ge(exp_made, i * NG + n + 1)
                    w = who[n - 2]
                    pe.wait_ge(taken[w], i * per_step[w] + (nth[n - 2] if n >= 2 else 0) + 1)
                    transpose_group(nc, c, t_ps[n % 2], probs[n % R], gs[n], turned)

                def feed(i, n):
                    g = gs[n]
                    if g.first:
                        pe.wait_ge(out_made, i * NU + g.ui + 1)
                    if n % (2 * NH) == 0:
                        pe.wait_ge(v_in[g.u.j], i * 16 + 16)
                    pe.wait_ge(taken[who[n]], i * per_step[who[n]] + nth[n] + 1)
                    values_group(nc, o_ps[g.ui % 2], pT[n % 4], v[g.u.j], g, 0 if v_shared else HD * g.u.hh, fed)

                with pe.Fori(0, steps) as i:
                    for k in range(LEAD):
                        score(i, k)
                    for n in range(NG):
                        turn(i, n)
                        if n % NH == NH - 1:
                            pe.sem_inc(heads_done, 1)
                        if n + LEAD < NG:
                            score(i, n + LEAD)
                        if n >= 2:
                            feed(i, n - 2)
                    for n in (NG - 2, NG - 1):
                        feed(i, n)

            def copy_out(eng, copy, i, n):
                eng.wait_ge(fed, i * NG + n + 1)
                eng.wait_ge(turned, i * NG + n + 1 + R)
                copy(pT[n % 4][:, 0:gs[n].m * P], t_ps[n % 2][:, 0:gs[n].m * P]).then_inc(taken[who[n]], 1)

            @block.scalar
            def _(act):
                act.sem_inc(fed, 4)

                def exponential(i, k):
                    g = gs[k]
                    u, us = g.u, g.ui % US
                    h4 = u.j * 2 + u.hh
                    if g.first:
                        act.wait_ge(max_made, i * NU + g.ui + 1)
                        if sink is not None:
                            nc.scalar.activation(esink[:, us:us + 1], sinks[:, h4:h4 + 1], ACT.Exp,
                                                 bias=nmx[:, us:us + 1])
                    e = probs[k % R][:, 0:g.m * P]
                    part = k - u.first
                    nc.scalar.activation(e, e, ACT.Exp, bias=nmx[:, us:us + 1], scale=scales[:, h4:h4 + 1],
                                         accum_out=rsum[:, us, part:part + 1]).then_inc(exp_made, 1)

                with act.Fori(0, steps) as i:
                    act.wait_ge(heads_set, i + 1)
                    for k in range(EXP_LEAD):
                        exponential(i, k)
                    for n in range(NG):
                        if who[n] == "s":
                            copy_out(act, nc.scalar.copy, i, n)
                        if n + EXP_LEAD < NG:
                            exponential(i, n + EXP_LEAD)
                        if n in (NG // 2 + 4, NG - 1):
                            j = n // (NG // 2 + 5)
                            act.wait_ge(pair_done, i * 2 + j + 3)
                            act.dma_start(y_out(i, j), gt[j][:]).then_inc(y_stored[j], 16)
                for j in range(2):
                    act.wait_ge(y_stored[j], 16 * (steps + 1))

            @block.vector
            def _(dve):
                dve.sem_inc(turned, R)

                with dve.Fori(0, steps) as i:
                    done = [0]

                    def link(ins):
                        done[0] += 1
                        ins.then_inc(chain, 1)
                        dve.wait_ge(chain, i * links + done[0])

                    def bias(k):
                        g = gs[k]
                        u, us = g.u, g.ui % US
                        part = k - u.first
                        dve.wait_ge(turned, i * NG + k + 1)
                        dve.wait_ge(scored, i * NG + k + 1)
                        nc.vector.memset(gate[:, k % US:k % US + 1], 0.0)
                        nc.vector.tensor_tensor_reduce(
                            out=probs[k % R][:, 0:g.m * P], in0=s_ps[k % 4][:, 0:g.m * P],
                            in1=bias_of(u)[:, g.a * P:(g.a + g.m) * P], scale=1.0, scalar=NEVER, op0=ALU.add,
                            op1=ALU.max, accum_out=mx[:, us, part:part + 1]).then_inc(biased, 1)
                        if not g.last:
                            return
                        dve.wait_ge(biased, i * NG + k + 5)
                        m0 = mx[:, us, 0:1]
                        if u.ng > 1:
                            m0 = top[:, us, 0:1]
                            link(nc.vector.tensor_reduce(m0, mx[:, us, 0:u.ng], AX_X, ALU.max))
                        scl = scales[:, u.j * 2 + u.hh:u.j * 2 + u.hh + 1]
                        if sink is not None:
                            link(nc.vector.tensor_scalar(top[:, us, 1:2], m0, scl,
                                                         sinks[:, u.j * 2 + u.hh:u.j * 2 + u.hh + 1],
                                                         ALU.mult, ALU.max))
                            nc.vector.tensor_scalar(nmx[:, us:us + 1], top[:, us, 1:2], -1.0, None,
                                                    ALU.mult).then_inc(max_made, 1)
                        else:
                            nc.vector.tensor_scalar(nmx[:, us:us + 1], m0, scl, -1.0, ALU.mult, ALU.mult
                                                    ).then_inc(max_made, 1)

                    def output(ui):
                        u, us = units[ui], ui % US
                        last = u.first + u.ng - 1
                        dve.wait_ge(exp_made, i * NG + last + 1)
                        d = rsum[:, us, 0:1]
                        if u.ng > 1:
                            d = den[:, us, 0:1]
                            link(nc.vector.reduce_sum(d, rsum[:, us, 0:u.ng], AX_X))
                        if sink is not None:
                            link(nc.vector.tensor_tensor(den[:, us, 1:2], d, esink[:, us:us + 1], ALU.add))
                            d = den[:, us, 1:2]
                        link(nc.vector.reciprocal(rden[:, us:us + 1], d))
                        if ui % (NU // 2) == 0:
                            dve.wait_ge(g_in[u.j], i * 16 + 16)
                        dve.wait_ge(fed, i * NG + last + 5)
                        cc = slice(HD * u.hh, HD * u.hh + HD)
                        nc.vector.scalar_tensor_tensor(
                            out=gt[u.j][:, u.b, cc], in0=o_ps[ui % 2][:, 0:HD], scalar=rden[:, us:us + 1],
                            in1=gt[u.j][:, u.b, cc], op0=ALU.mult, op1=ALU.mult).then_inc(out_made, 1)
                        if ui % (NU // 2) == NU // 2 - 1:
                            dve.wait_ge(out_made, i * NU + ui + 3)
                            dve.sem_inc(pair_done, 1)

                    if sink is not None:
                        nc.vector.tensor_copy(sinks[:], sink[:, bass.ds(i * 4, 4)])
                    nc.vector.tensor_copy(scales[:], scale_tab[:, bass.ds(i * 4, 4)]).then_inc(heads_set, 1)
                    dve.wait_ge(heads_set, i + 1)
                    for k in range(LEAD):
                        bias(k)
                    for n in range(NG + 3):
                        if n < NG and who[n] == "v":
                            copy_out(dve, nc.vector.tensor_copy, i, n)
                        if n + LEAD < NG:
                            bias(n + LEAD)
                        if n >= 3 and gs[n - 3].last:
                            output(gs[n - 3].ui)
                    assert done[0] == links


def stick_breaking(nc, c, fm, vals, gates, y_dram):
    steps = B_HEADS // 4
    units = [Unit(j, hh, b, list(range(b + 1))) for j in range(2) for hh in range(2) for b in range(NT)]
    gs = groups_of(units, latest_first=True)
    NG, NU, LEAD, R = len(gs), len(units), 6, 8
    assert NG % R == 0 and NU % 2 == 0
    who, nth, per_step = shares(NG, lambda k: k % 5 in (1, 3))
    with Scope(nc) as sc:
        qs = [sc.sb(f"qs{k}", [P, S], F32R) for k in range(2)]
        kh = [sc.sb(f"kh{k}", [P, S], F32R) for k in range(2)]
        kl = [sc.sb(f"kl{k}", [P, S], F32R) for k in range(2)]
        v = [sc.sb(f"v{k}", [P, NT, 2 * HD]) for k in range(2)]
        gt = [sc.sb(f"g{k}", [P, NT, 2 * HD]) for k in range(2)]
        beta = [sc.sb(f"beta{k}", [P, BANK]) for k in range(R)]
        keep = [sc.sb(f"keep{k}", [P, BANK]) for k in range(R)]
        left = [sc.sb(f"left{k}", [P, BANK + 8]) for k in range(R)]
        pT = [sc.sb(f"pT{k}", [P, BANK]) for k in range(4)]
        z_ps = [sc.ps(f"z{k}", [P, BANK]) for k in range(4)]
        t_ps = [sc.ps(f"t{k}", [P, BANK]) for k in range(2)]
        o_ps = [sc.ps(f"o{k}", [P, BANK]) for k in range(2)]
        head_in = sc.sems("head_in", 2)
        v_in = sc.sems("v_in", 2)
        g_in = sc.sems("g_in", 2)
        pair_done = sc.sem("pair_done")
        y_stored = sc.sems("y_stored", 2)
        heads_done = sc.sem("heads_done")
        scored = sc.sem("scored")
        squashed = sc.sem("squashed")
        edge = sc.sem("edge")
        scanned = sc.sem("scanned")
        weighed = sc.sem("weighed")
        turned = sc.sem("turned")
        taken = {"s": sc.sem("taken_s"), "v": sc.sem("taken_v")}
        fed = sc.sem("fed")
        out_made = sc.sem("out_made")
        NH = NG // 4

        with nc.Block() as block:
            @block.sync
            def _(sp):
                sp.sem_inc(pair_done, 2)
                sp.sem_inc(heads_done, 2)
                for j in range(2):
                    sp.sem_inc(y_stored[j], 16)
                with sp.Fori(0, steps) as i:
                    for j in range(2):
                        for hh in range(2):
                            qd, kd = (head_rows(fm, i, j, hh, FM0[name]) for name in ("qb", "kb"))
                            vd, gd = (token_view(d, (i * 2 + j) * P, P) for d in (vals, gates))
                            sp.wait_ge(heads_done, i * 4 + j * 2 + hh + 1)
                            if hh == 0:
                                sp.wait_ge(y_stored[j], i * 16 + 16)
                            load_head(sp, qs[hh], kh[hh], kl[hh], qd, kd, head_in[hh], S)
                            if hh == 0:
                                sp.dma_start(v[j][:], vd).then_inc(v_in[j], 16)
                                sp.dma_start(gt[j][:], gd).then_inc(g_in[j], 16)

            @block.tensor
            def _(pe):
                pe.sem_inc(squashed, 4)
                pe.sem_inc(taken["s"], 1)
                pe.sem_inc(taken["v"], 1)
                pe.sem_inc(out_made, 2)

                def score(i, k):
                    g = gs[k]
                    u, w = g.u, g.m * P
                    if k % NH == 0:
                        pe.wait_ge(head_in[u.hh], i * 192 + u.j * 96 + 96)
                    pe.wait_ge(squashed, i * NG + k + 1)
                    ins = score_group(nc, z_ps[k % 4][:, 0:w], qs[u.hh], kh[u.hh], kl[u.hh], u.b, g.a * P, w,
                                      stop=not g.first)
                    if g.first:
                        ins = nc.tensor.matmul(z_ps[k % 4][:, w - P:w], c.identb[:], c.causal[:],
                                               start=False, stop=True)
                    ins.then_inc(scored, 1)

                def turn(i, n):
                    pe.wait_ge(weighed, i * NG + n + 1 + R)
                    w = who[n - 2]
                    pe.wait_ge(taken[w], i * per_step[w] + (nth[n - 2] if n >= 2 else 0) + 1)
                    transpose_group(nc, c, t_ps[n % 2], beta[n % R], gs[n], turned)

                def feed(i, n):
                    g = gs[n]
                    if g.first:
                        pe.wait_ge(out_made, i * NU + g.ui + 1)
                    if n % (2 * NH) == 0:
                        pe.wait_ge(v_in[g.u.j], i * 16 + 16)
                    pe.wait_ge(taken[who[n]], i * per_step[who[n]] + nth[n] + 1)
                    values_group(nc, o_ps[g.ui % 2], pT[n % 4], v[g.u.j], g, HD * g.u.hh, fed)

                with pe.Fori(0, steps) as i:
                    for k in range(LEAD):
                        score(i, k)
                    for n in range(NG):
                        turn(i, n)
                        if n % NH == NH - 1:
                            pe.sem_inc(heads_done, 1)
                        if n + LEAD < NG:
                            score(i, n + LEAD)
                        if n >= 2:
                            feed(i, n - 2)
                    for n in (NG - 2, NG - 1):
                        feed(i, n)

            def copy_out(eng, copy, i, n):
                eng.wait_ge(fed, i * NG + n + 1)
                eng.wait_ge(turned, i * NG + n + 1 + R)
                copy(pT[n % 4][:, 0:gs[n].m * P], t_ps[n % 2][:, 0:gs[n].m * P]).then_inc(taken[who[n]], 1)

            @block.scalar
            def _(act):
                act.sem_inc(fed, 4)

                def squash(i, k):
                    w = gs[k].m * P
                    act.wait_ge(turned, i * NG + k + 1)
                    act.wait_ge(scored, i * NG + k + 1)
                    nc.scalar.activation(keep[k % R][:, 0:w], z_ps[k % 4][:, 0:w], ACT.Sigmoid, scale=-SCALE)
                    nc.scalar.activation(beta[k % R][:, 0:w], z_ps[k % 4][:, 0:w], ACT.Sigmoid, scale=SCALE
                                         ).then_inc(squashed, 1)

                with act.Fori(0, steps) as i:
                    for k in range(LEAD):
                        squash(i, k)
                    for n in range(NG):
                        if who[n] == "s":
                            copy_out(act, nc.scalar.copy, i, n)
                        if n + LEAD < NG:
                            squash(i, n + LEAD)
                        if n in (NG // 2 + 4, NG - 1):
                            j = n // (NG // 2 + 5)
                            act.wait_ge(pair_done, i * 2 + j + 3)
                            act.dma_start(token_view(y_dram, (i * 2 + j) * P + A_HEADS * HD, P), gt[j][:]
                                          ).then_inc(y_stored[j], 16)
                for j in range(2):
                    act.wait_ge(y_stored[j], 16 * (steps + 1))

            @block.gpsimd
            def _(pool):
                with pool.Fori(0, steps) as i:
                    for k, g in enumerate(gs):
                        w = g.m * P
                        pool.wait_ge(scanned, i * NG + k + 1)
                        nc.gpsimd.tensor_tensor(beta[k % R][:, 0:w], beta[k % R][:, 0:w], left[k % R][:, 1:w + 1],
                                                ALU.mult).then_inc(weighed, 1)

            @block.vector
            def _(dve):
                dve.sem_inc(turned, R)
                dve.sem_inc(weighed, R)

                with dve.Fori(0, steps) as i:
                    def scan(k):
                        g = gs[k]
                        w = g.m * P
                        dst = left[k % R]
                        dve.wait_ge(weighed, i * NG + k + 1)
                        if g.first:
                            ins = nc.vector.memset(dst[:, w:w + 1], 1.0)
                        else:
                            dve.wait_ge(scanned, i * NG + k)
                            ins = nc.vector.tensor_copy(dst[:, w:w + 1], left[(k - 1) % R][:, 0:1])
                        ins.then_inc(edge, 1)
                        dve.wait_ge(edge, i * NG + k + 1)
                        dve.wait_ge(squashed, i * NG + k + 5)
                        kr = keep[k % R][:, 0:w][:, ::-1]
                        nc.vector.tensor_tensor_scan(out=dst[:, 0:w][:, ::-1], data0=kr, data1=kr,
                                                     initial=dst[:, w:w + 1], op0=ALU.mult, op1=ALU.min
                                                     ).then_inc(scanned, 1)

                    def output(ui):
                        u = units[ui]
                        if ui % (NU // 2) == 0:
                            dve.wait_ge(g_in[u.j], i * 16 + 16)
                        dve.wait_ge(fed, i * NG + u.first + u.ng - 1 + 5)
                        cc = slice(HD * u.hh, HD * u.hh + HD)
                        nc.vector.tensor_tensor(gt[u.j][:, u.b, cc], o_ps[ui % 2][:, 0:HD], gt[u.j][:, u.b, cc],
                                                ALU.mult).then_inc(out_made, 1)
                        if ui % (NU // 2) == NU // 2 - 1:
                            dve.wait_ge(out_made, i * NU + ui + 3)
                            dve.sem_inc(pair_done, 1)

                    for k in range(LEAD - 1):
                        scan(k)
                    for n in range(NG + 3):
                        if n + LEAD - 1 < NG:
                            scan(n + LEAD - 1)
                        if n < NG and who[n] == "v":
                            copy_out(dve, nc.vector.tensor_copy, i, n)
                        if n >= 3 and gs[n - 3].last:
                            output(gs[n - 3].ui)


def index_scores(nc, c, fm, scores):
    units = [(j, hh, b, a, m) for j in range(2) for hh in range(2) for b in range(2, NT)
             for a, m in chunks(b + 1, PB)]
    NU = len(units)
    per_head = NU // 4
    steps = I_HEADS // 4
    assert NU % 4 == 0
    with Scope(nc) as sc:
        qs = [sc.sb(f"qs{k}", [P, S], F32R) for k in range(2)]
        kh = sc.sb("kh", [P, S], F32R)
        kl = sc.sb("kl", [P, S], F32R)
        w_rows = sc.sb("w_rows", [I_HEADS, 2, S])
        w = sc.sb("w", [P, NT, I_HEADS])
        pos = [sc.sb(f"pos{k}", [P, PIECE]) for k in range(4)]
        s_ps = [sc.ps(f"s{k}", [P, PIECE]) for k in range(4)]
        loaded = sc.sems("loaded", 2)
        keys_in = sc.sem("keys_in")
        w_in = sc.sem("w_in")
        w_sum = sc.sem("w_sum")
        w_turned = sc.sem("w_turned")
        w_made = sc.sem("w_made")
        scored = sc.sem("scored")
        clipped = sc.sem("clipped")
        added = sc.sem("added")
        with nc.Block() as block:
            @block.sync
            def _(sp):
                sp.dma_start(w_rows[:], fm[:, FM1["ki"] * P + HD:FM1["ki"] * P + HD + I_HEADS, :].rearrange(
                    "n h t -> h n t")).then_inc(w_in, 16)
                for r in range(2):
                    for t, d in ((kh, fm[0]), (kl, fm[1])):
                        sp.dma_start(t[r * HD:(r + 1) * HD, :].bitcast(F32), d[FM1["ki"] * P:FM1["ki"] * P + HD, :]
                                     ).then_inc(keys_in, 16)
                sp.sem_inc(scored, 2 * per_head)
                with sp.Fori(0, steps) as i:
                    for j in range(2):
                        for hh in range(2):
                            parts = head_rows(fm, i, j, hh, FM1["qi"])
                            sp.wait_ge(scored, i * NU + (j * 2 + hh + 1) * per_head)
                            for n, rows in enumerate(parts):
                                sp.dma_start(qs[hh][n * HD:(n + 1) * HD, :].bitcast(F32), rows).then_inc(loaded[hh], 16)

            @block.tensor
            def _(pe):
                pe.sem_inc(clipped, 4)
                pe.wait_ge(w_sum, 1)
                for t in range(NT):
                    last = nc.tensor.transpose(s_ps[0][:, t * I_HEADS:(t + 1) * I_HEADS],
                                               w_rows[:, 0, t * P:(t + 1) * P], c.ident[0:I_HEADS, 0:I_HEADS])
                last.then_inc(w_turned, 1)
                pe.wait_ge(w_made, 1)
                pe.wait_ge(keys_in, 64)
                with pe.Fori(0, steps) as i:
                    for ui, (j, hh, b, a, m) in enumerate(units):
                        if ui % per_head == 0:
                            pe.wait_ge(loaded[hh], i * 64 + j * 32 + 32)
                        pe.wait_ge(clipped, i * NU + ui + 1)
                        for x, wd in chunks(m * P, BANK):
                            last = score_group(nc, s_ps[ui % 4][:, x:x + wd], qs[hh], kh, kl, b, a * P + x, wd)
                        last.then_inc(scored, 1)

            @block.scalar
            def _(act):
                with act.Fori(0, steps) as i:
                    for ui, (j, hh, b, a, m) in enumerate(units):
                        act.wait_ge(scored, i * NU + ui + 1 + 2 * per_head)
                        act.wait_ge(added, i * NU + ui + 1 + per_head)
                        nc.scalar.activation(pos[ui % 4][:, 0:m * P], s_ps[ui % 4][:, 0:m * P], ACT.Relu
                                             ).then_inc(clipped, 1)

            @block.vector
            def _(dve):
                dve.wait_ge(w_in, 16)
                nc.vector.tensor_tensor(w_rows[:, 0, :], w_rows[:, 0, :], w_rows[:, 1, :], ALU.add
                                        ).then_inc(w_sum, 1)
                for b in range(2, NT):
                    nc.vector.memset(scores(b), 0.0)
                dve.wait_ge(w_turned, 1)
                nc.vector.tensor_scalar(w[:], s_ps[0][:, 0:NT * I_HEADS].rearrange("p (t n) -> p t n", t=NT),
                                        IDX_SCALE, None, ALU.mult).then_inc(w_made, 1)
                dve.wait_ge(w_made, 1)
                dve.sem_inc(added, 4 + per_head)
                with dve.Fori(0, steps) as i:
                    for ui, (j, hh, b, a, m) in enumerate(units):
                        dst = scores(b)[:, a * P:(a + m) * P]
                        dve.wait_ge(clipped, i * NU + ui + 5)
                        dve.wait_ge(added, i * NU + ui + 5)
                        nc.vector.scalar_tensor_tensor(
                            out=dst, in0=pos[ui % 4][:, 0:m * P],
                            scalar=w[:, b, bass.ds(i * 4 + j * 2 + hh, 1)], in1=dst, op0=ALU.mult, op1=ALU.add
                        ).then_inc(added, 1)


class Search:
    B0 = TOPK // P
    NB = NT - B0
    PER = 6

    def __init__(self, nc, sc, scores):
        self.nc, self.scores = nc, scores
        self.junk = [sc.sb(f"junk{k}", [P, S], U8) for k in range(2)]
        self.best, self.bit, self.cand, self.flip, self.thr, self.enough = (
            sc.sb(name, [P, self.NB], U32) for name in ("best", "bit", "cand", "flip", "thr", "enough"))
        self.cnt = sc.sb("cnt", [P, self.NB])
        self.ch = sc.sem("ch")
        self.counted = sc.sem("counted")

    def start(self, dve):
        v, ch = self.nc.vector, self.ch
        for b in range(self.B0, NT):
            v.memset(self.scores(b)[0:HD, b * P + HD:(b + 1) * P], NEVER)
        v.memset(self.best[:], 0)
        v.memset(self.bit[:], SIGN).then_inc(self.ch, 1)
        dve.wait_ge(ch, 1)

    def as_float(self, dve, base, src):
        v, ch = self.nc.vector, self.ch
        v.tensor_scalar(self.flip[:], src[:], 31, 0xFFFFFFFF, ALU.arith_shift_right, ALU.bitwise_xor
                        ).then_inc(ch, 1)
        dve.wait_ge(ch, base + 1)
        v.tensor_scalar(self.flip[:], self.flip[:], SIGN, None, ALU.bitwise_or).then_inc(ch, 1)
        dve.wait_ge(ch, base + 2)
        v.tensor_tensor(self.thr[:], src[:], self.flip[:], ALU.bitwise_xor).then_inc(ch, 1)
        dve.wait_ge(ch, base + 3)

    def bits(self, dve, first, last):
        v, ch, counted, PER, NB = self.nc.vector, self.ch, self.counted, self.PER, self.NB
        with dve.Fori(first, last) as i:
            v.tensor_tensor(self.cand[:], self.best[:], self.bit[:], ALU.bitwise_or).then_inc(ch, 1)
            dve.wait_ge(ch, i * PER + 2)
            self.as_float(dve, i * PER + 2, self.cand)
            for n in range(NB):
                b = n + self.B0
                if n >= 2:
                    dve.wait_ge(counted, i * NB + n - 1)
                v.tensor_scalar(self.junk[n % 2][:, 0:(b + 1) * P], self.scores(b),
                                self.thr[:, n:n + 1].bitcast(F32), None, ALU.is_ge, ALU.add,
                                accum_out=self.cnt[:, n:n + 1]).then_inc(counted, 1)
            dve.wait_ge(counted, i * NB + NB)
            v.tensor_scalar(self.enough[:], self.cnt[:], TOPK - 0.5, None, ALU.is_ge).then_inc(ch, 1)
            dve.wait_ge(ch, i * PER + 6)
            v.tensor_scalar(self.bit[:], self.bit[:], 1, None, ALU.logical_shift_right)
            v.copy_predicated(self.best[:], self.enough[:], self.cand[:]).then_inc(ch, 1)
            dve.wait_ge(ch, i * PER + 7)


def select_keys(nc, search, scores, neg_dist):
    B0, NB = search.B0, search.NB
    with Scope(nc) as sc:
        even = [sc.sb(f"even{k}", [P, S]) for k in range(2)]
        rank = [sc.sb(f"rank{k}", [P, S]) for k in range(2)]
        room = sc.sb("room", [P, NB])
        pre = sc.sem("pre")
        link = sc.sem("link")
        with nc.Block() as block:
            @block.vector
            def _(dve):
                v = nc.vector
                for b in range(B0):
                    L = (b + 1) * P
                    v.tensor_copy(scores(b), neg_dist[:, S - L:S]).then_inc(pre, 1)
                    dve.wait_ge(pre, b + 1)
                    v.memset(scores(b)[0:HD, L - HD:L], MASKED)
                search.as_float(dve, 32 * search.PER + 1, search.best)

                def stages(n):
                    L = (n + B0 + 1) * P
                    t = search.thr[:, n:n + 1].bitcast(F32)
                    sc_b, ev, rk = scores(n + B0), even[n % 2][:, 0:L], rank[n % 2][:, 0:L]

                    def count():
                        v.tensor_scalar(search.junk[n % 2][:, 0:L], sc_b, t, None, ALU.is_gt, ALU.add,
                                        accum_out=search.cnt[:, n:n + 1])
                        return v.tensor_scalar(ev, sc_b, t, None, ALU.is_equal)

                    def rank_equal():
                        v.tensor_scalar(room[:, n:n + 1], search.cnt[:, n:n + 1], -1.0, float(TOPK),
                                        ALU.mult, ALU.add)
                        return v.tensor_tensor_scan(out=rk, data0=ev, data1=ev, initial=0.0,
                                                    op0=ALU.add, op1=ALU.max)

                    def take():
                        return v.scalar_tensor_tensor(out=ev, in0=rk, scalar=room[:, n:n + 1], in1=ev,
                                                      op0=ALU.is_le, op1=ALU.mult)

                    def leave():
                        return v.scalar_tensor_tensor(out=rk, in0=sc_b, scalar=t, in1=ev,
                                                      op0=ALU.is_le, op1=ALU.subtract)

                    def bias():
                        return v.scalar_tensor_tensor(out=sc_b, in0=rk, scalar=MASKED, in1=neg_dist[:, S - L:S],
                                                      op0=ALU.mult, op1=ALU.add)

                    return [count, rank_equal, take, leave, bias]

                done = 0
                for n in range(0, NB, 2):
                    for pair in zip(stages(n), stages(n + 1)):
                        for stage in pair:
                            if done >= 2:
                                dve.wait_ge(link, done - 1)
                            stage().then_inc(link, 1)
                            done += 1


def out_project(nc, c, y_dram, w_out, resid, dst):
    KY = YW // P
    half = NT // 2
    WS = 4
    with Scope(nc) as sc:
        w = [sc.sb(f"w{k}", [P, D]) for k in range(WS)]
        wh = sc.sb("wh", [P, KY, D], F32R)
        wl = sc.sb("wl", [P, KY, D], F32R)
        y = [sc.sb(f"y{k}", [P, YW]) for k in range(2)]
        x = [sc.sb(f"x{k}", [P, D]) for k in range(2)]
        h = [sc.sb(f"h{k}", [P, D]) for k in range(2)]
        yTh = [sc.sb(f"yTh{k}", [P, YW], F32R) for k in range(2)]
        yTl = [sc.sb(f"yTl{k}", [P, YW], F32R) for k in range(2)]
        t_ps = sc.ps("t", [P, 3 * BANK])
        o_ps = [sc.ps(f"o{k}", [P, D]) for k in range(2)]
        w_in = sc.sems("w_in", WS)
        w_hi = sc.sem("w_hi")
        w_split = sc.sem("w_split")
        hi_made = sc.sem("hi_made")
        y_in = sc.sems("y_in", 2)
        x_in = sc.sems("x_in", 2)
        turned = sc.sem("turned")
        taken = sc.sem("taken")
        summed = sc.sem("summed")
        added = sc.sem("added")
        stored = sc.sems("stored", 2)
        with nc.Block() as block:
            @block.sync
            def _(sp):
                sp.sem_inc(w_split, WS)

                def load(n, k, d, to, arrived):
                    sp.dma_start(to[k][:], d[bass.ds(n * P, P), :]).then_inc(arrived[k], 16)

                def store(n, k):
                    sp.dma_start(dst[bass.ds(n * P, P), :], h[k][:]).then_inc(stored[k], 16)

                for k in range(2):
                    load(k, k, y_dram, y, y_in)
                    load(k, k, resid, x, x_in)
                for j in range(KY):
                    sp.wait_ge(w_split, j + 1)
                    sp.dma_start(w[j % WS][:], w_out[j * P:(j + 1) * P, :]).then_inc(w_in[j % WS], 16)
                with sp.Fori(0, half - 1) as i:
                    for k in range(2):
                        n = i * 2 + k + 2
                        sp.wait_ge(turned, n + 1)
                        load(n, k, y_dram, y, y_in)
                        sp.wait_ge(added, n + 1)
                        load(n, k, resid, x, x_in)
                        store(n - 2, k)
                for k in range(2):
                    sp.wait_ge(added, NT + k + 1)
                    store(NT - 2 + k, k)
                    sp.wait_ge(stored[k], 16 * (half + 1))

            @block.tensor
            def _(pe):
                pe.sem_inc(turned, 2)
                pe.sem_inc(taken, 1)

                def turn(i, k):
                    pe.wait_ge(y_in[k], i * 16 + 16)
                    pe.wait_ge(taken, i * 2 + k + 1)
                    for j in range(KY):
                        last = nc.tensor.transpose(t_ps[:, j * P:(j + 1) * P], y[k][:, j * P:(j + 1) * P], c.ident[:])
                    last.then_inc(turned, 1)

                def product(i, k):
                    pe.wait_ge(taken, i * 2 + k + 2)
                    pe.wait_ge(added, i * 2 + k + 1)
                    sta = [(yTh[k][:, j * P:(j + 1) * P], yTl[k][:, j * P:(j + 1) * P]) for j in range(KY)]
                    for x0 in range(0, D, BANK):
                        split_matmuls(nc, o_ps[k][:, x0:x0 + BANK], sta,
                                      [(wh[:, j, x0:x0 + BANK], wl[:, j, x0:x0 + BANK]) for j in range(KY)], summed)

                turn(0, 0)
                pe.wait_ge(w_split, KY + WS)
                with pe.Fori(0, half - 1) as i:
                    turn(i, 1)
                    product(i, 0)
                    turn(i + 1, 0)
                    product(i, 1)
                turn(half - 1, 1)
                product(half - 1, 0)
                product(half - 1, 1)

            @block.scalar
            def _(act):
                act.sem_inc(summed, 4)
                for j in range(KY):
                    act.wait_ge(w_in[j % WS], 16 * (j // WS + 1))
                    nc.scalar.copy(wh[:, j, :], w[j % WS][:]).then_inc(w_hi, 1)
                with act.Fori(0, half) as i:
                    for k in range(2):
                        n = i * 2 + k
                        act.wait_ge(summed, n * 2 + 2)
                        act.wait_ge(turned, n + 3)
                        nc.scalar.copy(yTh[k][:], t_ps[:, 0:YW]).then_inc(hi_made, 1)

            @block.vector
            def _(dve):
                dve.sem_inc(added, 2)
                for k in range(2):
                    dve.sem_inc(stored[k], 16)
                for j in range(KY):
                    dve.wait_ge(w_hi, j + 1)
                    nc.vector.tensor_tensor(wl[:, j, :], w[j % WS][:], wh[:, j, :].bitcast(F32), ALU.subtract
                                            ).then_inc(w_split, 1)

                def low_part(i, k):
                    dve.wait_ge(hi_made, i * 2 + k + 1)
                    nc.vector.tensor_tensor(yTl[k][:], t_ps[:, 0:YW], yTh[k][:].bitcast(F32), ALU.subtract
                                            ).then_inc(taken, 1)

                def residual(i, k):
                    n = i * 2 + k
                    dve.wait_ge(summed, n * 2 + 6)
                    dve.wait_ge(x_in[k], i * 16 + 16)
                    dve.wait_ge(stored[k], i * 16 + 16)
                    nc.vector.tensor_tensor(h[k][:], o_ps[k][:], x[k][:], ALU.add).then_inc(added, 1)

                low_part(0, 0)
                with dve.Fori(0, half - 1) as i:
                    low_part(i, 1)
                    residual(i, 0)
                    low_part(i + 1, 0)
                    residual(i, 1)
                low_part(half - 1, 1)
                residual(half - 1, 0)
                residual(half - 1, 1)


def head_rows(fm, i, j, hh, tile):
    return [fm[n, bass.ds((i * 2 + j + tile) * P + hh * HD, HD), :] for n in range(2)]


def memory_kv(nc, c, mem, gain, w_fm, w_v, km, vm):
    with Scope(nc) as sc:
        memT = [sc.sb(f"memT{n}", [P, D // P, MEM], F32R) for n in range(2)]
        norm_rows(nc, c, mem, gain, MEM, D, dstT=memT)
        project(nc, [[t] for t in memT], D // P, MEM, w_fm, 2, c.fm_one, km, [(w_v, vm, 2 * P, False)])


def token_view(d, col, w):
    return d.rearrange("(t p) n -> p t n", p=P)[:, :, bass.ds(col, w)]


def memory_attention(nc, c, fm, km, vm, gm, y, ycol):
    def loads(i, j, hh):
        pair = i * 2 + j
        return (head_rows(fm, i, j, hh, FM0["qm"]), head_rows(km, i, j, hh, 0),
                token_view(vm, pair * P, P), token_view(gm, pair * P, P))

    softmax_attention(nc, c, 1, [(b, [0, 1]) for b in range(NT)], loads, MEM,
                      lambda i, j: token_view(y, (i * 2 + j) * P + ycol, P), c.scale_m, None,
                      lambda u: c.zero_bias[:])


def trunk(nc, a, out):
    def dram(name, shape):
        return nc.dram_tensor(name, shape, F32, kind="Internal").ap()

    def parts(name, shape):
        return dram(name, (2,) + shape)

    x, mem = a["x"][0], a["mem"][0]
    fm0, fm1 = parts("fm0", (NFM * P, S)), parts("fm1", (NFM * P, S))
    va, ga = dram("va", (S, P)), dram("ga", (S, A_HEADS * HD))
    vb, gb = dram("vb", (S, B_HEADS * HD)), dram("gb", (S, B_HEADS * HD))
    gm0, gm1 = dram("gm0", (S, M_HEADS * HD)), dram("gm1", (S, M_HEADS * HD))
    km0, km1 = parts("km0", (MEM, MEM)), parts("km1", (MEM, MEM))
    vm0, vm1 = dram("vm0", (MEM, MEM)), dram("vm1", (MEM, MEM))
    late_dram = [dram(f"late{k}", (P, D // P, HT)) for k in range(2)]
    y0, y1 = dram("y0", (S, YW)), dram("y1", (S, YW))
    h1, h2 = dram("h1", (S, D)), dram("h2", (S, D))
    ckv, gc = dram("ckv", (S, LAT)), dram("gc", (S, C_HEADS * HD))
    kc, vc = parts("kc", (C_HEADS * HD, S)), dram("vc", (S, C_HEADS * HD))

    def wide(w, c0, od, width, silu=False):
        return [(w[:, c0 + a:c0 + a + n], od[:, a:a + n], n, silu) for a, n in chunks(width, 2 * P)]

    with Scope(nc) as top:
        c = make_constants(nc, top, a["e_sinks"])

        memory_kv(nc, c, mem, a["e_mem_norm"], a["e_mem_k"], a["e_w_mem_kv"][0][:, MEM:2 * MEM], km0, vm0)
        memory_kv(nc, c, mem, a["o_mem_norm"], a["o_mem_k"], a["o_w_mem_kv"][0][:, MEM:2 * MEM], km1, vm1)
        with Scope(nc) as sc:
            hT = [sc.sb(f"hT{n}", [P, D // P, S], F32R) for n in range(2)]
            norm_rows(nc, c, x, a["e_norm"], S, D, dstT=hT)
            w = a["e_w_in"][0]
            project(nc, [[t] for t in hT], D // P, S, a["e_fm"], NFM, c.fm_scale0, fm0,
                    wide(w, 640, va, 128) + wide(w, 768, ga, 512, True) + wide(w, 2304, vb, 512)
                    + wide(w, 2816, gb, 512, True) + wide(w, 3584, gm0, 256, True))

        def loads_a(i, j, hh):
            return (head_rows(fm0, i, j, hh, FM0["qa"]),
                    [fm0[n, bass.ds(i * HD + FM0["ka"] * P, HD), :] for n in range(2)],
                    token_view(va, i * HD, HD), token_view(ga, (i * 2 + j) * P, P))

        softmax_attention(nc, c, 2, [(b, list(range(max(b - 1, 0), b + 1))) for b in range(NT)], loads_a, S,
                          lambda i, j: token_view(y0, (i * 2 + j) * P, P), c.slope_a, c.sink,
                          lambda u: c.window[:, 0 if u.b else P:2 * P], v_shared=True)
        stick_breaking(nc, c, fm0, vb, gb, y0)
        memory_attention(nc, c, fm0, km0, vm0, gm0, y0, (A_HEADS + B_HEADS) * HD)
        out_project(nc, c, y0, a["e_w_out"][0], x, h1)

        w, scale, QC = a["o_w_in"][0], c.fm_scale1, FM1["qc"]
        early = Scope(nc)
        hT = [early.sb(f"hT{k}", [P, D // P, HT], F32R, side="right") for k in range(2)]
        with Scope(nc) as sc:
            late = [sc.sb(f"late{k}", [P, D // P, HT], F32R) for k in range(2)]
            norm_rows(nc, c, h1[0:HT, :], a["o_norm"], HT, D, dstT=hT)
            norm_rows(nc, c, h1[HT:S, :], a["o_norm"], HT, D, dstT=late)
            project(nc, list(zip(hT, late)), D // P, S, a["o_fm"][0:QC], QC, scale[:, 0:QC], fm1[:, 0:QC * P, :],
                    [], keep=[(d, t[:].bitcast(F32)) for d, t in zip(late_dram, late)])
        with Scope(nc) as sc:
            all_scores = sc.sb("scores", [P, P * (NT * (NT + 1) // 2)])

            def scores(b):
                o = P * (b * (b + 1) // 2)
                return all_scores[:, o:o + (b + 1) * P]

            index_scores(nc, c, fm1, scores)
            with Scope(nc) as sel:
                search = Search(nc, sel, scores)

                def rest(half, beside, fetch=()):
                    at = slice(half * HT, (half + 1) * HT)
                    project(nc, [[t] for t in hT], D // P, HT, a["o_fm"][QC:NFM], NFM - QC, scale[:, QC:NFM],
                            fm1[:, QC * P:NFM * P, at],
                            wide(w, 1024, ckv[at, :], LAT) + wide(w, 1864, gc[at, :], 1024, True)
                            + wide(w, 3144, gm1[at, :], 256, True), beside=beside, fetch=fetch)

                def search_first(dve):
                    search.start(dve)
                    search.bits(dve, 0, BITS1)

                rest(0, search_first)
                rest(1, lambda dve: search.bits(dve, BITS1, BITS2),
                     fetch=[(t[:].bitcast(F32), d) for t, d in zip(hT, late_dram)])
                early.close()
                with Scope(nc) as part:
                    cT = [part.sb(f"cT{k}", [P, LAT // P, S], F32R) for k in range(2)]
                    norm_rows(nc, c, ckv, a["o_kv_norm"], S, LAT, dstT=cT)
                    uv = a["o_w_uv"][0].rearrange("l h d -> l (h d)")
                    project(nc, [[t] for t in cT], LAT // P, S, a["o_uk"], 8, c.fm_one, kc, wide(uv, 0, vc, 1024),
                            beside=lambda dve: search.bits(dve, BITS2, 32))
                memory_attention(nc, c, fm1, km1, vm1, gm1, y1, C_HEADS * HD)
                with Scope(nc) as part:
                    neg_dist = part.sb("neg_dist", [P, S])
                    distances(nc, neg_dist, S)
                    select_keys(nc, search, scores, neg_dist)

            def loads_c(i, j, hh):
                pair = i * 2 + j
                return (head_rows(fm1, i, j, hh, FM1["qc"]), head_rows(kc, i, j, hh, 0),
                        token_view(vc, pair * P, P), token_view(gc, pair * P, P))

            softmax_attention(nc, c, C_HEADS // 4, [(b, list(range(b + 1))) for b in range(NT)], loads_c, S,
                              lambda i, j: token_view(y1, (i * 2 + j) * P, P), c.slope_c, None,
                              lambda u: scores(u.b))
        out_project(nc, c, y1, a["o_w_out"][0], h1, h2)
        norm_rows(nc, c, h2, a["final_norm"].rearrange("(a n) -> a n", a=1), S, D, out=out[0])


def tiles(w, starts):
    import numpy as np
    return np.ascontiguousarray(np.stack([w[:, s:s + P].reshape(-1, P, P).transpose(1, 0, 2) for s in starts]))


def kernel(**inputs):
    import numpy as _np
    import concourse.bacc as _bacc
    from concourse import mybir as _mybir
    from concourse.bass_utils import run_bass_kernel_spmd as _run

    nc = _bacc.Bacc("TRN2", target_bir_lowering=False, num_devices=1)
    arrays = {k: _np.ascontiguousarray(v) for k, v in inputs.items()}
    e, o = arrays["e_w_in"][0], arrays["o_w_in"][0]
    arrays["e_fm"] = tiles(e, [0, 128, 256, 384, 512] + list(range(1280, 2304, 128)) + [3328, 3456])
    arrays["o_fm"] = tiles(o, list(range(1280, 1793, 128)) + list(range(0, 1024, 128)) + [2888, 3016])
    arrays["e_mem_k"] = tiles(arrays["e_w_mem_kv"][0], [0, 128])
    arrays["o_mem_k"] = tiles(arrays["o_w_mem_kv"][0], [0, 128])
    arrays["o_uk"] = tiles(arrays.pop("o_w_uk")[0].reshape(LAT, C_HEADS * HD), list(range(0, 1024, 128)))
    aps = {k: nc.dram_tensor("in_" + k, v.shape, _mybir.dt.from_np(v.dtype), kind="ExternalInput").ap()
           for k, v in arrays.items()}
    out = nc.dram_tensor("out_0", (1, S, D), _mybir.dt.float32, kind="ExternalOutput").ap()
    trunk(nc, aps, out)
    r = _run(nc, [{"in_" + k: v for k, v in arrays.items()}], core_ids=[0])
    return r.results[0]["out_0"]
```
